# Optimizing a Trainium2 kernel written in Bass

```python
import jax, jax.numpy as jnp
from jax import lax
import numpy as np

D_MODEL = 1024
BATCH = 1
SEQ = 1024
DEPTH = 1

CHUNK = 64
EPS = 1e-6

GDN_HEADS = 8
GDN_DK = 64
GDN_DV = 64
CONV_K = 4
GDN_QK = GDN_HEADS * GDN_DK
GDN_V = GDN_HEADS * GDN_DV
GDN_CONV_W = 2 * GDN_QK + GDN_V

FOX_HEADS = 8
FOX_DH = 64
FOX_W = FOX_HEADS * FOX_DH
Q_BLOCK = 128

N_BRANCH = 2
SPLIT_SIZES = (GDN_CONV_W, GDN_V, GDN_HEADS, GDN_HEADS,
               FOX_W, FOX_W, FOX_W, FOX_W, FOX_HEADS,
               N_BRANCH * D_MODEL)
D_IN = sum(SPLIT_SIZES)

kernel_name = "hybrid_gdn_fox_gated_merge"

def rmsnorm(x, w):
    xf = x.astype(jnp.float32)
    y = xf * lax.rsqrt(jnp.mean(xf * xf, axis=-1, keepdims=True) + EPS)
    return (y * w.astype(jnp.float32)).astype(x.dtype)

def l2norm(x):
    return x * lax.rsqrt(jnp.sum(x * x, axis=-1, keepdims=True) + EPS)

def causal_depthwise_conv(x, w):
    c = x.shape[-1]
    return lax.conv_general_dilated(
        x, w[:, None, :].astype(x.dtype), window_strides=(1,),
        padding=[(CONV_K - 1, 0)], dimension_numbers=('NWC', 'WIO', 'NWC'),
        feature_group_count=c)

def gated_deltanet(qkv, z, b_logit, a_logit, conv_w, a_log, dt_bias, norm_w):
    B, S, _ = qkv.shape
    H, C = GDN_HEADS, CHUNK
    n = S // C
    dtype = qkv.dtype
    qkv = jax.nn.silu(causal_depthwise_conv(qkv, conv_w)).astype(jnp.float32)
    q, k, v = jnp.split(qkv, [GDN_QK, 2 * GDN_QK], axis=-1)
    q = l2norm(q.reshape(B, S, H, GDN_DK)) * (GDN_DK ** -0.5)
    k = l2norm(k.reshape(B, S, H, GDN_DK))
    v = v.reshape(B, S, H, GDN_DV)
    beta = jax.nn.sigmoid(b_logit.astype(jnp.float32))
    g = -jnp.exp(a_log.astype(jnp.float32)) * jax.nn.softplus(
        a_logit.astype(jnp.float32) + dt_bias.astype(jnp.float32))

    def chunkify(t):
        return t.reshape(B, n, C, H, -1).transpose(0, 3, 1, 2, 4)

    q, k, v = chunkify(q), chunkify(k), chunkify(v)
    beta = beta.reshape(B, n, C, H).transpose(0, 3, 1, 2)
    g = jnp.cumsum(g.reshape(B, n, C, H).transpose(0, 3, 1, 2), axis=-1)

    causal = jnp.tril(jnp.ones((C, C), dtype=bool))
    strict = jnp.tril(jnp.ones((C, C), dtype=bool), -1)
    diff = g[..., :, None] - g[..., None, :]
    decay = jnp.exp(jnp.where(causal, diff, -jnp.inf))

    kb = k * beta[..., None]
    vb = v * beta[..., None]
    m_low = jnp.where(strict, jnp.einsum('bhnid,bhnjd->bhnij', kb, k) * decay, 0.0)
    eye = jnp.eye(C, dtype=jnp.float32)
    t_inv = lax.linalg.triangular_solve(
        m_low + eye, jnp.broadcast_to(eye, m_low.shape),
        left_side=True, lower=True, unit_diagonal=True)
    w_val = jnp.einsum('bhnij,bhnjd->bhnid', t_inv, vb)
    k_cum = jnp.einsum('bhnij,bhnjd->bhnid', t_inv, kb * jnp.exp(g)[..., None])
    a_qk = jnp.einsum('bhnid,bhnjd->bhnij', q, k) * decay
    q_g = q * jnp.exp(g)[..., None]
    k_tail = k * jnp.exp(g[..., -1:] - g)[..., None]
    g_last = jnp.exp(g[..., -1])

    def step(state, xs):
        w_c, kc_c, qg_c, a_c, kt_c, gl_c = xs
        u = w_c - jnp.einsum('bhcd,bhde->bhce', kc_c, state)
        o = jnp.einsum('bhcd,bhde->bhce', qg_c, state) + jnp.einsum('bhij,bhje->bhie', a_c, u)
        state = state * gl_c[..., None, None] + jnp.einsum('bhcd,bhce->bhde', kt_c, u)
        return state, o

    mv = lambda t: jnp.moveaxis(t, 2, 0)
    state0 = jnp.zeros((B, H, GDN_DK, GDN_DV), jnp.float32)
    _, o = lax.scan(step, state0, (mv(w_val), mv(k_cum), mv(q_g), mv(a_qk), mv(k_tail), mv(g_last)))
    o = o.transpose(1, 0, 3, 2, 4).reshape(B, S, H, GDN_DV)
    zh = z.reshape(B, S, H, GDN_DV).astype(jnp.float32)
    y = rmsnorm(o, norm_w) * jax.nn.silu(zh)
    return y.reshape(B, S, GDN_V).astype(dtype)

def forgetting_attention(q, k, v, z, f_logit, f_bias, qn_w, kn_w, on_w):
    B, S, _ = q.shape
    H, dh = FOX_HEADS, FOX_DH
    nb = S // Q_BLOCK
    dtype = q.dtype
    qh = rmsnorm(q.reshape(B, S, H, dh), qn_w).transpose(0, 2, 1, 3)
    kh = rmsnorm(k.reshape(B, S, H, dh), kn_w).transpose(0, 2, 1, 3)
    vh = v.reshape(B, S, H, dh).transpose(0, 2, 1, 3)
    log_f = jax.nn.log_sigmoid(f_logit.astype(jnp.float32) + f_bias.astype(jnp.float32))
    c = lax.cumsum(log_f, axis=1).transpose(0, 2, 1)
    q_blocks = qh.reshape(B, H, nb, Q_BLOCK, dh).transpose(2, 0, 1, 3, 4)
    c_blocks = c.reshape(B, H, nb, Q_BLOCK).transpose(2, 0, 1, 3)
    key_pos = jnp.arange(S)
    scale = dh ** -0.5

    def block(args):
        qb, cb, i = args
        q_pos = i * Q_BLOCK + jnp.arange(Q_BLOCK)
        s = jnp.einsum('bhqd,bhkd->bhqk', qb, kh).astype(jnp.float32) * scale
        s = s + cb[..., :, None] - c[..., None, :]
        s = jnp.where(key_pos[None, :] <= q_pos[:, None], s, -jnp.inf)
        p = jax.nn.softmax(s, axis=-1)
        return jnp.einsum('bhqk,bhkd->bhqd', p.astype(vh.dtype), vh)

    o = lax.map(block, (q_blocks, c_blocks, jnp.arange(nb)))
    o = o.transpose(1, 0, 3, 2, 4).reshape(B, S, H, dh)
    zh = z.reshape(B, S, H, dh).astype(jnp.float32)
    y = rmsnorm(o.astype(jnp.float32), on_w) * jax.nn.silu(zh)
    return y.reshape(B, S, FOX_W).astype(dtype)

def setup_inputs(seed: int = 0) -> dict:
    key = jax.random.key(seed)
    ks = jax.random.split(key, 20)
    f32 = jnp.float32
    nrm = lambda k, shape, scale: jax.random.normal(k, shape, f32) * scale
    gain = lambda k, shape: 1.0 + 0.02 * jax.random.normal(k, shape, f32)
    dt = jnp.exp(jax.random.uniform(ks[5], (DEPTH, GDN_HEADS), f32,
                                    math_log(0.001), math_log(0.1)))
    return {
        'x': jax.random.normal(ks[0], (BATCH, SEQ, D_MODEL), f32),
        'norm_w': gain(ks[1], (DEPTH, D_MODEL)),
        'w_in': nrm(ks[2], (DEPTH, D_MODEL, D_IN), D_MODEL ** -0.5),
        'gate_b': nrm(ks[3], (DEPTH, N_BRANCH * D_MODEL), 0.02),
        'conv_w': nrm(ks[4], (DEPTH, CONV_K, GDN_CONV_W), CONV_K ** -0.5),
        'a_log': jnp.log(jax.random.uniform(ks[6], (DEPTH, GDN_HEADS), f32, 1.0, 16.0)),
        'dt_bias': dt + jnp.log(-jnp.expm1(-dt)),
        'gdn_norm_w': gain(ks[7], (DEPTH, GDN_DV)),
        'f_bias': 2.0 + 0.1 * jax.random.normal(ks[8], (DEPTH, FOX_HEADS), f32),
        'fox_qn_w': gain(ks[9], (DEPTH, FOX_DH)),
        'fox_kn_w': gain(ks[10], (DEPTH, FOX_DH)),
        'fox_on_w': gain(ks[11], (DEPTH, FOX_DH)),
        'w_up_gdn': nrm(ks[12], (DEPTH, GDN_V, D_MODEL), GDN_V ** -0.5),
        'w_up_fox': nrm(ks[13], (DEPTH, FOX_W, D_MODEL), FOX_W ** -0.5),
        'w_out': nrm(ks[14], (DEPTH, D_MODEL, D_MODEL), D_MODEL ** -0.5),
        'final_norm_w': gain(ks[15], (D_MODEL,)),
    }

def math_log(v):
    return float(np.log(v))

def reference(x, norm_w, w_in, gate_b, conv_w, a_log, dt_bias, gdn_norm_w, f_bias,
              fox_qn_w, fox_kn_w, fox_on_w, w_up_gdn, w_up_fox, w_out, final_norm_w):
    split_points = [int(s) for s in np.cumsum(SPLIT_SIZES)[:-1]]
    for l in range(DEPTH):
        h = rmsnorm(x, norm_w[l])
        proj = jnp.einsum('bsd,de->bse', h, w_in[l])
        (gdn_qkv, gdn_z, gdn_b, gdn_a, fox_q, fox_k, fox_v, fox_z, fox_f,
         gate_logit) = jnp.split(proj, split_points, axis=-1)
        y_a = gated_deltanet(gdn_qkv, gdn_z, gdn_b, gdn_a, conv_w[l], a_log[l],
                             dt_bias[l], gdn_norm_w[l])
        y_b = forgetting_attention(fox_q, fox_k, fox_v, fox_z, fox_f, f_bias[l],
                                   fox_qn_w[l], fox_kn_w[l], fox_on_w[l])
        gates = jax.nn.sigmoid(gate_logit + gate_b[l])
        g_a, g_b = jnp.split(gates, 2, axis=-1)
        merged = (g_a * jnp.einsum('bsc,cd->bsd', y_a, w_up_gdn[l])
                  + g_b * jnp.einsum('bsc,cd->bsd', y_b, w_up_fox[l]))
        x = x + jnp.einsum('bsd,de->bse', merged, w_out[l])
    return rmsnorm(x, final_norm_w)


_drawn_inputs = setup_inputs


def setup_inputs(seed=0):
    import zlib

    import numpy as np

    out = dict(_drawn_inputs(seed))
    spreads = {}
    factors = {'norm_w': 3.235,
     'gate_b': 8.0,
     'gdn_norm_w': 8.0,
     'f_bias': 3.153,
     'fox_qn_w': 8.0,
     'fox_kn_w': 8.0,
     'fox_on_w': 8.0,
     'final_norm_w': 2.86}
    for name, (base, spread) in spreads.items():
        noise = np.random.default_rng([zlib.crc32(name.encode()), seed]).standard_normal(out[name].shape)
        drawn = base * np.exp(spread * noise) if base else spread * noise
        out[name] = __import__('jax').numpy.asarray(drawn.astype(out[name].dtype))
    for name, factor in factors.items():
        out[name] = (out[name] * factor).astype(out[name].dtype)
    return out
```

```python
from contextlib import ExitStack

import concourse.bass as bass
from concourse import mybir

F32 = mybir.dt.float32
F32R = mybir.dt.float32r
I32 = mybir.dt.int32
ALU = mybir.AluOpType
ACT = mybir.ActivationFunctionType
ds = bass.ds

P = 128
HALF = 512
EPS = 1e-6
NEG = -1e30
LN_MAX = 1e18
DH = 64
LEVELS = (2, 4, 8, 16, 32)


def program(nc, x, norm_w, w_in, gate_b, conv_w, a_log, dt_bias, gdn_norm_w, f_bias,
            fox_qn_w, fox_kn_w, fox_on_w, w_up_gdn, w_up_fox, w_out, final_norm_w, out, dbg=None):
    _, S, D = x.shape
    H = a_log.shape[1]
    KT = D // P
    NT = S // P
    PAIRS = H // 2
    CONV = conv_w.shape[1]
    QKV = conv_w.shape[2]
    HW = H * DH
    COL_Z = QKV
    COL_B = COL_Z + HW
    COL_A = COL_B + H
    COL_FOX = COL_A + H
    COL_F = COL_FOX + 4 * HW
    COL_GATE = COL_F + H
    QKV_T = QKV // P
    N_GDN = QKV_T + PAIRS
    N_FOX = 4 * PAIRS
    assert S == 2 * HALF and NT == 8 and KT == 8 and PAIRS == 4 and QKV_T == 12

    w_view = w_in[0].rearrange("(k p) n -> p k n", p=P)
    up_view = [w_up_gdn[0].rearrange("(k p) n -> p k n", p=P), w_up_fox[0].rearrange("(k p) n -> p k n", p=P)]
    rows_dram = nc.dram_tensor("rows_scratch", [3, H, S], F32, kind="Internal").ap()
    y_dram = nc.dram_tensor("y_scratch", [PAIRS * P, S], F32, kind="Internal").ap()
    m_dram = nc.dram_tensor("m_scratch", [D, S], F32, kind="Internal").ap()
    fox_dram = nc.dram_tensor("fox_scratch", [N_FOX * P, S], F32, kind="Internal").ap()

    ctx = ExitStack()
    with ctx:
        def sem(name):
            return ctx.enter_context(nc.semaphore(name))

        def sb(name, shape, dt=F32, where=ctx):
            return where.enter_context(nc.sbuf_tensor(name, shape, dt))

        pj = ctx.enter_context(nc.psum_tensor("pj", [P, 2, HALF], F32))
        pa = ctx.enter_context(nc.psum_tensor("pa", [P, 2, HALF], F32))
        pb = ctx.enter_context(nc.psum_tensor("pb", [P, 2, HALF], F32))
        pc = ctx.enter_context(nc.psum_tensor("pc", [P, 2, HALF], F32))

        h_hi = sb("h_hi", [P, KT, S], F32R)
        h_lo = sb("h_lo", [P, KT, S], F32R)
        w_raw = sb("w_raw", [P, 2, KT, P])
        w_hi = sb("w_hi", [P, 2, KT, P], F32R)
        w_lo = sb("w_lo", [P, 2, KT, P], F32R)
        ident = sb("ident", [P, P])
        blk_ones = sb("blk_ones", [P, P])
        cst = sb("cst", [P, P])
        vecs = sb("vecs", [P, 16])
        eps_t = vecs[:, 0:1]
        gdn_nw = vecs[:, 1:2]
        fox_nw = {"q": vecs[:, 2:3], "k": vecs[:, 3:4], "o": vecs[:, 4:5]}
        sgn, bias_raw, bias_s, alog_raw, coef = (vecs[:, 5 + n:6 + n] for n in range(5))
        toks = sb("toks", [P, 6, NT, H])
        lnb_tok, g_tok, c_tok, b_tok, bg_tok, kt_tok = (toks[:, n] for n in range(6))

        consts_loaded = sem("consts_loaded")
        w_loaded = [sem("w_loaded0"), sem("w_loaded1")]
        w_hi_done = sem("w_hi_done")
        w_ready = sem("w_ready")
        pj_done = sem("pj_done")
        pj_free = sem("pj_free")
        passed = sem("passed")
        SMALL_DMAS = 3

        def alone(eng):
            eng.sem_inc(passed, 1)

        def load_w(sp, m, col, slot):
            if not (isinstance(m, int) and m < 2):
                sp.wait_ge(w_ready, m - 1)
            sp.dma_start(w_raw[:, slot], w_view[:, :, ds(col, P)]).then_inc(w_loaded[slot], 16)

        def loads_of(m2, slot):
            return 16 * (m2 + 1) + (16 * (SMALL_DMAS - 1) if slot == 0 else 0)

        def split_hi(act, m, m2, slot):
            act.wait_ge(w_loaded[slot], loads_of(m2, slot))
            if not (isinstance(m, int) and m < 2):
                act.wait_ge(pj_done, 2 * (m - 1))
            nc.scalar.activation(w_hi[:, slot], w_raw[:, slot], ACT.Copy).then_inc(w_hi_done, 1)

        def split_lo(dve, m, slot):
            dve.wait_ge(w_hi_done, m + 1)
            nc.vector.tensor_tensor(w_lo[:, slot], w_raw[:, slot], w_hi[:, slot].bitcast(F32),
                                    ALU.subtract).then_inc(w_ready, 1)

        def project(pe, n, slot, half, k, banks=2):
            if k == 0:
                if half == 0:
                    pe.wait_ge(w_ready, n + 1)
                pe.wait_ge(pj_free, 2 * n + half + 3 - banks)
            o = pj[:, half * (banks - 1)]
            cols = slice(HALF * half, HALF * half + HALF)
            nc.tensor.matmul(o, w_hi[:, slot, k], h_hi[:, k, cols], start=(k == 0), stop=False)
            nc.tensor.matmul(o, w_hi[:, slot, k], h_lo[:, k, cols], start=False, stop=False)
            last = nc.tensor.matmul(o, w_lo[:, slot, k], h_hi[:, k, cols], start=False, stop=(k == KT - 1))
            if k == KT - 1:
                last.then_inc(pj_done, 1)


        def project_up(pe, q, slot, half, k, y_hi, y_lo, o, up_hi, up_lo):
            if k == 0:
                if half == 0:
                    pe.wait_ge(up_ready, q + 1)
                pe.wait_ge(up_free, 2 * q + half)
            cols = slice(HALF * half, HALF * half + HALF)
            nc.tensor.matmul(o, up_hi[:, slot, k], y_hi[:, k, cols], start=(k == 0), stop=False)
            nc.tensor.matmul(o, up_hi[:, slot, k], y_lo[:, k, cols], start=False, stop=False)
            last = nc.tensor.matmul(o, up_lo[:, slot, k], y_hi[:, k, cols], start=False, stop=(k == PAIRS - 1))
            if k == PAIRS - 1:
                last.then_inc(up_done, 1)

        mask_m = sb("mask_m", [P, P])
        mask_a = sb("mask_a", [P, P])
        neg_m1 = sb("neg_m1", [P, P])
        lev = sb("lev", [P, len(LEVELS), P], I32)
        gl = sb("gl", [P, 2, NT * H])
        outer = ctx.enter_context(ExitStack())
        qkv = sb("qkv", [P, QKV_T, S], where=outer)
        zg = sb("zg", [P, PAIRS, S], where=outer)
        st = outer.enter_context(ExitStack())
        xc = sb("xc", [P, CONV - 1 + S], where=st)
        ebuf = sb("ebuf", [P, S], where=st)
        sq = sb("sq", [P, S], where=st)
        rst = sb("rst", [P, S], where=st)
        crow = sb("crow", [P, S], where=st)
        rb_row = sb("rb_row", [P, S], where=st)
        rows_in = sb("rows_in", [P, P], where=st)
        stat = sb("stat", [P, 2], where=st)
        e_last = sb("e_last", [P, 2, P], where=st)
        xt, xs, nw_bc = qkv[:, 0:2], qkv[:, 2:4], qkv[:, 4]
        u_row, e_row, sp_row, keep_row = (zg[:, n] for n in range(4))

        sbm = sb("sbm", [P, 2, P], where=st)
        levf = sb("levf", [P, len(LEVELS) + 1, P], where=st)

        masks = sem("masks")
        masks_done = sem("masks_done")
        small_zeroed = sem("small_zeroed")
        rows_zeroed = sem("rows_zeroed")
        x_loaded = [sem("x_loaded0"), sem("x_loaded1")]
        nw_loaded = sem("nw_loaded")
        rstd_step = sem("rstd_step")
        xs_done = sem("xs_done")
        x_turned = sem("x_turned")
        h_hi_done = sem("h_hi_done")
        h_done = sem("h_done")
        cst_turned = sem("cst_turned")
        vec_step = sem("vec_step")
        alog_exp = sem("alog_exp")
        row_act = sem("row_act")
        row_dve = sem("row_dve")
        rows_stored = sem("rows_stored")
        tok_turned = sem("tok_turned")
        tok_dve = sem("tok_dve")
        tok_act = sem("tok_act")
        last_picked = sem("last_picked")
        conv_step = sem("conv_step")
        exp_done = sem("exp_done")
        silu_step = sem("silu_step")
        sq_done = sem("sq_done")
        ssq_done = sem("ssq_done")
        norm_act = sem("norm_act")
        qk_normed = sem("qk_normed")
        NV = 8

        with nc.Block() as block:
            @block.sync
            def _(sp):
                sp.wait_ge(small_zeroed, 1)
                sp.dma_start(w_raw[:, 0, :, 0:H], w_view[:, :, COL_B:COL_B + H]).then_inc(w_loaded[0], 16)
                sp.dma_start(w_raw[:, 0, :, 32:32 + H], w_view[:, :, COL_A:COL_A + H]).then_inc(w_loaded[0], 16)
                sp.dma_start(w_raw[:, 0, :, 64:64 + H], w_view[:, :, COL_F:COL_F + H]).then_inc(w_loaded[0], 16)
                load_w(sp, 1, 0, 1)
                for j in range(2):
                    sp.dma_start(xt[:, j], x[0, P * j:P * j + P, :]).then_inc(x_loaded[j], 16)
                sp.wait_ge(rows_zeroed, 1)
                sp.dma_start(rows_in[0:CONV * QKV_T, :],
                               conv_w[0].rearrange("k (m p) -> (k m) p", p=P)).then_inc(consts_loaded, 16)
                sp.dma_start(rows_in[64:64 + 2 * KT, :],
                               gate_b[0].rearrange("(m p) -> m p", p=P)).then_inc(consts_loaded, 16)
                with sp.Fori(0, NT // 2 - 1) as i:
                    for j in range(2):
                        sp.wait_ge(xs_done, 2 * i + j + 1)
                        sp.dma_start(xt[:, j], x[0, ds((2 * i + j + 2) * P, P), :]).then_inc(x_loaded[j], 16)
                with sp.Fori(0, N_GDN // 2 - 1) as i:
                    for j in range(2):
                        load_w(sp, 2 * i + j + 2, (2 * i + j + 1) * P, j)
                load_w(sp, N_GDN, (N_GDN - 1) * P, 0)
                load_w(sp, N_GDN + 1, COL_FOX, 1)
                sp.wait_ge(row_dve, 6)
                for n, rows in enumerate((crow[32:32 + H], rb_row[32:32 + H], crow[64:64 + H])):
                    to = rows_dram[n].rearrange("(b a) s -> a b s", b=2) if n < 2 else rows_dram[n]
                    sp.dma_start(to, rows).then_inc(rows_stored, 16)
                sp.wait_ge(rows_stored, 48)

            @block.gpsimd
            def _(pool):
                made = [0]

                def link(ins):
                    made[0] += 1
                    ins.then_inc(masks, 1)
                    pool.wait_ge(masks, made[0])

                nc.gpsimd.memset(w_raw[:, 0], 0.0).then_inc(small_zeroed, 1)
                nc.gpsimd.memset(rows_in[:, :], 0.0).then_inc(rows_zeroed, 1)
                link(nc.gpsimd.memset(ident[:, :], 0.0))
                link(nc.gpsimd.affine_select(ident[:, :], ident[:, :], pattern=[[-1, P]], base=0,
                                             channel_multiplier=1, compare_op=ALU.not_equal, fill=1.0))
                link(nc.gpsimd.memset(mask_a[:, :], 0.0))
                link(nc.gpsimd.affine_select(mask_m[:, :], mask_a[:, :], pattern=[[1, P]], base=0,
                                             channel_multiplier=-1, compare_op=ALU.is_gt, fill=NEG))
                link(nc.gpsimd.affine_select(mask_a[:, :], mask_a[:, :], pattern=[[1, P]], base=0,
                                             channel_multiplier=-1, compare_op=ALU.is_ge, fill=NEG))
                link(nc.gpsimd.memset(mask_m[0:DH, DH:P], NEG))
                link(nc.gpsimd.memset(mask_a[0:DH, DH:P], NEG))
                link(nc.gpsimd.memset(e_last[:, :, :], 0.0))
                for c in range(2):
                    link(nc.gpsimd.affine_select(e_last[:, c], e_last[:, c], pattern=[[0, P]],
                                                 base=-(DH * c + DH - 1), channel_multiplier=1,
                                                 compare_op=ALU.not_equal, fill=1.0))

                def same_block(dst, b):
                    v = dst.rearrange("p (n b) -> p n b", b=b)
                    link(nc.gpsimd.memset(dst, 1.0))
                    link(nc.gpsimd.affine_select(v, v, pattern=[[-b, P // b], [0, b]], base=0,
                                                 channel_multiplier=1, compare_op=ALU.is_ge, fill=0.0))
                    link(nc.gpsimd.affine_select(v, v, pattern=[[b, P // b], [0, b]], base=b - 1,
                                                 channel_multiplier=-1, compare_op=ALU.is_ge, fill=0.0))

                same_block(sbm[:, 0], 1)
                for n, b in enumerate((1,) + LEVELS):
                    small, large = sbm[:, n % 2], sbm[:, (n + 1) % 2]
                    same_block(large, 2 * b)
                    link(nc.gpsimd.tensor_tensor(levf[:, n], large, small, ALU.subtract))
                    link(nc.gpsimd.affine_select(levf[:, n], levf[:, n], pattern=[[1, P]], base=0,
                                                 channel_multiplier=-1, compare_op=ALU.is_gt, fill=0.0))
                same_block(blk_ones[:, :], DH)
                link(nc.gpsimd.tensor_scalar(neg_m1[:, :], levf[:, 0], -1.0, None, ALU.mult))
                nc.gpsimd.tensor_copy(lev[:, :, :], levf[:, 1:len(LEVELS) + 1]).then_inc(masks_done, 1)

            @block.scalar
            def _(act):
                nc.scalar.preload_act_table_set("natural_log_exp_and_others")
                act.sem_inc(pj_free, 2)
                act.dma_start(nw_bc, norm_w[0, :].partition_broadcast(P)).then_inc(nw_loaded, 16)
                act.wait_ge(vec_step, 1)
                for dst, src in ((gdn_nw[0:DH], gdn_norm_w), (gdn_nw[DH:P], gdn_norm_w),
                                 (fox_nw["q"][0:DH], fox_qn_w), (fox_nw["q"][DH:P], fox_qn_w),
                                 (fox_nw["k"][0:DH], fox_kn_w), (fox_nw["k"][DH:P], fox_kn_w),
                                 (fox_nw["o"][0:DH], fox_on_w), (fox_nw["o"][DH:P], fox_on_w),
                                 (bias_raw[32:32 + H], dt_bias), (bias_raw[64:64 + H], f_bias),
                                 (alog_raw[32:32 + H], a_log)):
                    act.dma_start(dst, src[0].rearrange("(p o) -> p o", o=1)).then_inc(consts_loaded, 16)
                act.wait_ge(vec_step, 2)
                with act.Fori(0, NT // 2) as i:
                    for j in range(2):
                        act.wait_ge(x_loaded[j], 16 * i + 16)
                        act.wait_ge(x_turned, 4 * i)
                        nc.scalar.activation(xs[:, j], xt[:, j], ACT.Square,
                                             accum_out=stat[:, j:j + 1]).then_inc(rstd_step, 1)
                        act.wait_ge(rstd_step, 6 * i + 3 * j + 1)
                        nc.scalar.activation(stat[:, j:j + 1], stat[:, j:j + 1], ACT.Ln, bias=eps_t,
                                             scale=1.0 / D).then_inc(rstd_step, 1)
                        act.wait_ge(rstd_step, 6 * i + 3 * j + 2)
                        nc.scalar.activation(stat[:, j:j + 1], stat[:, j:j + 1], ACT.Exp,
                                             scale=-0.5).then_inc(rstd_step, 1)
                    for j in range(2):
                        for b in range(2):
                            act.wait_ge(x_turned, 4 * i + 2 * j + b + 1)
                            nc.scalar.activation(h_hi[:, 4 * b:4 * b + 4, ds((2 * i + j) * P, P)],
                                                 pa[:, b].rearrange("p (k c) -> p k c", c=P),
                                                 ACT.Copy).then_inc(h_hi_done, 1)
                split_hi(act, 0, 0, 0)
                split_hi(act, 1, 0, 1)
                act.wait_ge(consts_loaded, 16 * 13)
                nc.scalar.activation(coef, alog_raw, ACT.Exp).then_inc(alog_exp, 1)
                act.wait_ge(vec_step, 10)
                for half in range(2):
                    act.wait_ge(pj_done, half + 1)
                    nc.scalar.activation(u_row[:, HALF * half:HALF * half + HALF], pj[:, half], ACT.Identity,
                                         bias=bias_s, scale=sgn).then_inc(pj_free, 1)
                act.wait_ge(pj_free, 4)
                nc.scalar.activation(e_row, u_row, ACT.Abs).then_inc(row_act, 1)
                act.wait_ge(row_act, 1)
                nc.scalar.activation(e_row, e_row, ACT.Exp, scale=-1.0).then_inc(row_act, 1)
                act.wait_ge(row_act, 2)
                nc.scalar.activation(e_row, e_row, ACT.Ln, bias=1.0).then_inc(row_act, 1)

                def sigmoid_act(n):
                    act.wait_ge(silu_step, 2 * (n - 1) + 1)
                    nc.scalar.activation(ebuf[:, :], ebuf[:, :], ACT.Ln).then_inc(exp_done, 1)
                    act.wait_ge(exp_done, 3 * (n - 1) + 2)
                    nc.scalar.activation(ebuf[:, :], ebuf[:, :], ACT.Exp, scale=-1.0).then_inc(exp_done, 1)

                def take_qkv(n, slot, m2, split=True):
                    act.wait_ge(conv_step, CONV * (n - 1))
                    for half in range(2):
                        act.wait_ge(pj_done, 2 * n + half + 1)
                        nc.scalar.activation(xc[:, CONV - 1 + HALF * half:CONV - 1 + HALF * half + HALF],
                                             pj[:, half], ACT.Copy).then_inc(pj_free, 1)
                    split_hi(act, n + 1, m2, 1 - slot)
                    act.wait_ge(conv_step, CONV * n)
                    act.wait_ge(silu_step, 2 * (n - 1))
                    nc.scalar.activation(ebuf[:, :], qkv[:, ds(n - 1, 1)].rearrange("p a s -> p (a s)"),
                                         ACT.Exp, scale=-1.0).then_inc(exp_done, 1)
                    sigmoid_act(n)

                def take_z(n, slot, m2):
                    act.wait_ge(silu_step, 2 * (n - 1))
                    for half in range(2):
                        act.wait_ge(pj_done, 2 * n + half + 1)
                        nc.scalar.activation(xc[:, CONV - 1 + HALF * half:CONV - 1 + HALF * half + HALF],
                                             pj[:, half], ACT.Copy).then_inc(pj_free, 1)
                    split_hi(act, n + 1, m2, 1 - slot)
                    act.wait_ge(pj_free, 2 * n + 4)
                    nc.scalar.activation(ebuf[:, :], xc[:, CONV - 1:], ACT.Exp, scale=-1.0).then_inc(exp_done, 1)
                    sigmoid_act(n)

                def squares(j):
                    act.wait_ge(ssq_done, 1 * j)
                    nc.scalar.activation(sq[:, :], qkv[:, ds(j, 1)].rearrange("p a s -> p (a s)"),
                                         ACT.Square).then_inc(sq_done, 1)

                def norms(j):
                    act.wait_ge(ssq_done, j + 1)
                    act.wait_ge(qk_normed, 1 * j)
                    nc.scalar.activation(rst[:, :], pa[:, :, :].rearrange("p a s -> p (a s)"), ACT.Ln,
                                         bias=eps_t).then_inc(norm_act, 1)
                    act.wait_ge(norm_act, 2 * j + 1)
                    nc.scalar.activation(rst[:, :], rst[:, :], ACT.Exp, scale=-0.5).then_inc(norm_act, 1)

                with act.Fori(0, 2 * PAIRS // 2) as i:
                    for j in range(2):
                        take_qkv(2 * i + j + 1, 1 - j, i + 1 if j == 0 else i + 1, True)
                act.wait_ge(silu_step, 2 * 2 * PAIRS)
                with act.Fori(0, PAIRS // 2) as i:
                    for j in range(2):
                        squares(2 * i + j)
                        take_qkv(2 * i + j + 1 + 2 * PAIRS, 1 - j, i + 1 + PAIRS)
                        norms(2 * i + j)
                act.wait_ge(tok_dve, 4)
                nc.scalar.activation(b_tok, lnb_tok, ACT.Exp).then_inc(tok_act, 1)
                nc.scalar.activation(bg_tok, bg_tok, ACT.Exp).then_inc(tok_act, 1)
                act.wait_ge(tok_dve, 6)
                nc.scalar.activation(kt_tok, kt_tok, ACT.Exp).then_inc(tok_act, 1)
                nc.scalar.activation(gl[:, :, :], pc[:, 0, 0:2 * NT * H].rearrange("p (c n) -> p c n", c=2),
                                     ACT.Exp).then_inc(tok_act, 1)
                with act.Fori(0, PAIRS // 2) as i:
                    for j in range(2):
                        squares(2 * i + j + PAIRS)
                        take_z(2 * i + j + 1 + 3 * PAIRS, 1 - j, i + 1 + PAIRS + PAIRS // 2)
                        norms(2 * i + j + PAIRS)

            @block.vector
            def _(dve):
                nc.vector.memset(vecs[:, :], 0.0).then_inc(vec_step, 1)
                dve.wait_ge(vec_step, 1)
                nc.vector.memset(eps_t, EPS).then_inc(vec_step, 1)
                nc.vector.memset(sgn, -1.0)
                nc.vector.memset(xc[:, 0:CONV - 1], 0.0).then_inc(vec_step, 1)
                dve.wait_ge(vec_step, 3)
                nc.vector.memset(sgn[32:64], 1.0).then_inc(vec_step, 1)
                nc.vector.memset(keep_row, 1.0).then_inc(vec_step, 1)
                dve.wait_ge(vec_step, 5)
                nc.vector.memset(keep_row[0:32], 0.0)
                nc.vector.memset(keep_row[32:64].rearrange("p (n c) -> p n c", c=DH)[:, :, 0:1],
                                 0.0).then_inc(vec_step, 1)
                dve.sem_inc(h_done, 2)
                dve.wait_ge(nw_loaded, 16)
                with dve.Fori(0, NT // 2) as i:
                    for j in range(2):
                        dve.wait_ge(rstd_step, 6 * i + 3 * j + 3)
                        nc.vector.scalar_tensor_tensor(xs[:, j], xt[:, j], stat[:, j:j + 1], nw_bc,
                                                       ALU.mult, ALU.mult).then_inc(xs_done, 1)
                    for j in range(2):
                        for b in range(2):
                            cols = ds((2 * i + j) * P, P)
                            dve.wait_ge(h_hi_done, 4 * i + 2 * j + b + 1)
                            nc.vector.tensor_tensor(h_lo[:, 4 * b:4 * b + 4, cols],
                                                    pa[:, b].rearrange("p (k c) -> p k c", c=P),
                                                    h_hi[:, 4 * b:4 * b + 4, cols].bitcast(F32),
                                                    ALU.subtract).then_inc(h_done, 1)
                split_lo(dve, 0, 0)
                split_lo(dve, 1, 1)
                dve.wait_ge(cst_turned, 1)
                nc.vector.tensor_copy(cst[:, :], pc[:, 1, 0:P]).then_inc(vec_step, 1)
                dve.wait_ge(consts_loaded, 16 * 13)
                nc.vector.tensor_tensor(bias_s, bias_raw, sgn, ALU.mult).then_inc(vec_step, 1)
                dve.wait_ge(alog_exp, 1)
                nc.vector.tensor_scalar(coef, coef, -1.0, None, ALU.mult).then_inc(vec_step, 1)
                nc.vector.tensor_scalar(fox_nw["q"], fox_nw["q"], -(DH ** -0.5), None, ALU.mult).then_inc(vec_step, 1)
                dve.wait_ge(vec_step, 10)
                dve.wait_ge(row_act, 3)
                nc.vector.scalar_tensor_tensor(sp_row, u_row, 0.0, e_row, ALU.max, ALU.add).then_inc(row_dve, 1)
                dve.wait_ge(row_dve, 1)
                nc.vector.tensor_scalar(sp_row, sp_row, coef, None, ALU.mult).then_inc(row_dve, 1)
                dve.wait_ge(row_dve, 2)
                nc.vector.tensor_tensor_scan(crow[:, :], keep_row, sp_row, 0.0, ALU.mult,
                                             ALU.add).then_inc(row_dve, 1)
                dve.wait_ge(row_dve, 3)
                nc.vector.tensor_copy(rb_row[32:64], crow[0:32]).then_inc(row_dve, 1)
                dve.wait_ge(row_dve, 4)
                nc.vector.tensor_tensor(rb_row[32:64], rb_row[32:64], crow[32:64], ALU.add).then_inc(row_dve, 2)

                def conv(n, slot):
                    split_lo(dve, n + 1, 1 - slot)
                    dve.wait_ge(pj_free, 2 * n + 4)
                    y = qkv[:, ds(n - 1, 1)].rearrange("p a s -> p (a s)")
                    for d in range(CONV):
                        tap = cst[:, ds((CONV - 1 - d) * QKV_T + n - 1, 1)]
                        src = xc[:, CONV - 1 - d:CONV - 1 - d + S]
                        if d == 0:
                            nc.vector.tensor_scalar(y, src, tap, None, ALU.mult).then_inc(conv_step, 1)
                        else:
                            dve.wait_ge(conv_step, CONV * (n - 1) + d)
                            nc.vector.scalar_tensor_tensor(y, src, tap, y, ALU.mult, ALU.add).then_inc(conv_step, 1)
                    sigmoid(n)
                    nc.vector.tensor_tensor(y, y, ebuf[:, :], ALU.mult).then_inc(silu_step, 1)

                def sigmoid(n):
                    dve.wait_ge(exp_done, 3 * (n - 1) + 1)
                    nc.vector.tensor_scalar(ebuf[:, :], ebuf[:, :], LN_MAX, 1.0, ALU.min, ALU.add).then_inc(silu_step, 1)
                    dve.wait_ge(exp_done, 3 * n)

                def normed(j):
                    dve.wait_ge(norm_act, 2 * j + 2)
                    t = qkv[:, ds(j, 1)].rearrange("p a s -> p (a s)")
                    nc.vector.tensor_tensor(t, t, rst[:, :], ALU.mult).then_inc(qk_normed, 1)

                with dve.Fori(0, 2 * PAIRS // 2) as i:
                    for j in range(2):
                        conv(2 * i + j + 1, 1 - j)
                with dve.Fori(0, PAIRS // 2) as i:
                    for j in range(2):
                        conv(2 * i + j + 1 + 2 * PAIRS, 1 - j)
                        normed(2 * i + j)
                dve.wait_ge(tok_turned, 1)
                for n, row in enumerate((0, 32, 64)):
                    nc.vector.tensor_copy(toks[:, n], pb[:, :, :].rearrange("p a (t r) -> p (a t) r", r=P)
                                          [:, :, row:row + H]).then_inc(tok_dve, 1)
                dve.wait_ge(tok_dve, 3)
                nc.vector.tensor_tensor(bg_tok, lnb_tok, g_tok, ALU.add).then_inc(tok_dve, 1)
                dve.wait_ge(last_picked, 1)
                for c in range(2):
                    rows = slice(DH * c, DH * c + DH)
                    nc.vector.tensor_tensor(kt_tok[rows], pc[rows, 0, NT * H * c:NT * H * (c + 1)].rearrange("p (t h) -> p t h", h=H),
                                            g_tok[rows], ALU.subtract).then_inc(tok_dve, 1)
                with dve.Fori(0, PAIRS // 2) as i:
                    for j in range(2):
                        n = 2 * i + j + 1 + 3 * PAIRS
                        split_lo(dve, n + 1, j)
                        sigmoid(n)
                        nc.vector.scalar_tensor_tensor(zg[:, ds(2 * i + j, 1)].rearrange("p a s -> p (a s)"),
                                                       xc[:, CONV - 1:], gdn_nw, ebuf[:, :],
                                                       ALU.mult, ALU.mult).then_inc(silu_step, 1)
                        normed(2 * i + j + PAIRS)

            @block.tensor
            def _(pe):
                pe.wait_ge(masks_done, 1)
                pe.wait_ge(rows_zeroed, 1)
                pe.wait_ge(consts_loaded, 16 * 13)
                nc.tensor.transpose(pc[:, 1, 0:P], rows_in[:, :], ident[:, :]).then_inc(cst_turned, 1)
                with pe.Fori(0, NT // 2) as i:
                    for j in range(2):
                        pe.wait_ge(xs_done, 2 * i + j + 1)
                        for b in range(2):
                            pe.wait_ge(h_done, 4 * i + 2 * j + b + 1)
                            for k in range(4):
                                last = nc.tensor.transpose(pa[:, b, k * P:(k + 1) * P],
                                                           xs[:, j, (4 * b + k) * P:(4 * b + k + 1) * P], ident[:, :])
                            last.then_inc(x_turned, 1)
                pe.wait_ge(h_done, 2 * NT + 2)

                def project_tile(n, slot):
                    for half in range(2):
                        for k in range(KT):
                            project(pe, n, slot, half, k)

                def head_sums(j):
                    pe.wait_ge(sq_done, j + 1)
                    pe.wait_ge(norm_act, 2 * j)
                    for half in range(2):
                        last = nc.tensor.matmul(pa[:, half], blk_ones[:, :], sq[:, HALF * half:HALF * half + HALF],
                                                start=True, stop=True)
                    last.then_inc(ssq_done, 1)

                project_tile(0, 0)
                with pe.Fori(0, 2 * PAIRS // 2) as i:
                    for j in range(2):
                        project_tile(2 * i + j + 1, 1 - j)
                pe.wait_ge(row_dve, 6)
                for t in range(NT):
                    last = nc.tensor.transpose(pb[:, t // 4, (t % 4) * P:(t % 4 + 1) * P], crow[:, P * t:P * t + P],
                                               ident[:, :])
                last.then_inc(tok_turned, 1)
                with pe.Fori(0, PAIRS // 2) as i:
                    for j in range(2):
                        project_tile(2 * i + j + 1 + 2 * PAIRS, 1 - j)
                        head_sums(2 * i + j)
                pe.wait_ge(tok_dve, 4)
                pe.wait_ge(vec_step, 7)
                for c in range(2):
                    last = nc.tensor.matmul(pc[:, 0, NT * H * c:NT * H * (c + 1)], e_last[:, c],
                                            g_tok.rearrange("p t h -> p (t h)"), start=True, stop=True)
                last.then_inc(last_picked, 1)
                with pe.Fori(0, PAIRS // 2) as i:
                    for j in range(2):
                        project_tile(2 * i + j + 1 + 3 * PAIRS, 1 - j)
                        head_sums(2 * i + j + PAIRS)

        st.close()
        if dbg == 1:
            return dump(nc, out, [qkv[:, m] for m in range(QKV_T)] + [zg[:, m] for m in range(PAIRS)] +
                        [toks[:, n].rearrange("p t h -> p (t h)") for n in range(6)] + [gl[:, :, :].rearrange("p c n -> p (c n)")])

        st = outer.enter_context(ExitStack())
        rbm = sb("rbm", [P, H, P], where=st)
        gbm = sb("gbm", [P, H, P], where=st)
        rt = sb("rt", [P, H, P], where=st)
        tt = sb("tt", [P, H, P], where=st)
        xsb = sb("xsb", [P, H, P], where=st)
        kfix = sb("kfix", [P, PAIRS, P], where=st)
        qfix = sb("qfix", [P, PAIRS, P], where=st)
        vfix = sb("vfix", [P, PAIRS, P], where=st)
        qg = sb("qg", [P, PAIRS, P], where=st)
        kbg = sb("kbg", [P, H, DH], where=st)
        ktail = sb("ktail", [P, H, DH], where=st)
        vb = sb("vb", [P, H, DH], where=st)
        kct = sb("kct", [P, PAIRS, P], where=st)
        wu = sb("wu", [P, H, DH], where=st)
        u = sb("u", [P, H, DH], where=st)
        state = sb("state", [P, PAIRS, P], where=st)
        fst = sb("fst", [P, 2, HALF], where=st)
        oq = xsb[:, 0:4]
        osq = xsb[:, 4:8]
        ors = xsb[:, 0:4]
        o_t = wu[:, :, :].rearrange("p (a b) d -> p a (b d)", b=2)

        rb_loaded = sem("rb_loaded")
        gb_loaded = sem("gb_loaded")
        tile_copied = sem("tile_copied")
        rb_pool = sem("rb_pool")
        gb_pool = sem("gb_pool")
        eg_done = sem("eg_done")
        decay_done = sem("decay_done")
        kv_turned = sem("kv_turned")
        kv_scaled = sem("kv_scaled")
        qg_done = sem("qg_done")
        kk_mm = sem("kk_mm")
        qk_mm = sem("qk_mm")
        m_done = sem("m_done")
        a_done = sem("a_done")
        r_step = sem("r_step")
        t_done = sem("t_done")
        mt_mm = sem("mt_mm")
        mt_out = sem("mt_out")
        rr_mm = sem("rr_mm")
        kw_mm = sem("kw_mm")
        kw_out = sem("kw_out")
        ks_mm = sem("ks_mm")
        qs_mm = sem("qs_mm")
        su_mm = sem("su_mm")
        au_mm = sem("au_mm")
        u_done = sem("u_done")
        s_step = sem("s_step")
        state_zero = sem("state_zero")
        oq_out = sem("oq_out")
        o_step = sem("o_step")
        osq_done = sem("osq_done")
        ossq_mm = sem("ossq_mm")
        ors_done = sem("ors_done")
        fox_out = sem("fox_out")
        fox_stored = [sem("fox_stored0"), sem("fox_stored1")]
        NL = len(LEVELS)
        N2 = N_GDN + 1
        GRP = H // 2

        def place(h):
            return GRP * (h % 2) + h // 2

        def per_head(rows, t):
            return rows.rearrange("p t h -> p (t h)")[:, ds(t * H, H)].unsqueeze(2)

        with nc.Block() as block:
            @block.sync
            def _(sp):
                def step(t, last_col):
                    sp.wait_ge(mt_mm, 2 * NL * t)
                    sp.dma_start(rbm[:, :, :], rows_dram[1, :, ds(t * P, P)].partition_broadcast(P)).then_inc(rb_loaded, 16)
                    load_w(sp, N2 + 1 + 2 * t, COL_FOX + P + 2 * P * t, 0)
                    sp.wait_ge(au_mm, 1 * t)
                    alone(sp)
                    sp.dma_start(gbm[:, :, :], rows_dram[0, :, ds(t * P, P)].partition_broadcast(P)).then_inc(gb_loaded, 16)
                    load_w(sp, N2 + 2 + 2 * t, last_col, 1)

                with sp.Fori(0, NT - 1) as t:
                    step(t, COL_FOX + 2 * P + 2 * P * t)
                step(NT - 1, COL_GATE)

            @block.gpsimd
            def _(pool):
                def by_parity(buf):
                    return buf[:, :, :].rearrange("p (b a) c -> p b a c", b=2)

                with pool.Fori(0, NT) as t:
                    tok_by_parity = g_tok.rearrange("p t h -> p (t h)")[:, ds(t * H, H)].rearrange(
                        "p (a b) -> p b a", b=2).unsqueeze(3).broadcast_to([P, 2, GRP, P])
                    pool.wait_ge(qk_mm, 2 * t)
                    pool.wait_ge(qg_done, 2 * t)
                    for n, dst in ((1, kfix), (2, vfix), (0, qfix)):
                        nc.gpsimd.tensor_copy(dst[:, :, :], qkv[:, PAIRS * n:PAIRS * (n + 1), ds(t * P, P)]).then_inc(tile_copied, 1)
                    pool.wait_ge(rb_loaded, 16 * t + 16)
                    nc.gpsimd.tensor_tensor(by_parity(rbm), by_parity(rbm), tok_by_parity,
                                            ALU.subtract).then_inc(rb_pool, 1)
                    pool.wait_ge(rb_pool, 2 * t + 1)
                    nc.gpsimd.tensor_tensor(rbm[:, :, :], rbm[:, :, :],
                                            mask_m[:, :].unsqueeze(1).broadcast_to([P, H, P]), ALU.add).then_inc(rb_pool, 1)
                    pool.wait_ge(eg_done, t + 1)
                    alone(pool)
                    nc.gpsimd.tensor_tensor(by_parity(gbm), by_parity(gbm), tok_by_parity,
                                            ALU.subtract).then_inc(gb_pool, 1)
                    pool.wait_ge(gb_pool, 2 * t + 1)
                    nc.gpsimd.tensor_tensor(gbm[:, :, :], gbm[:, :, :],
                                            mask_a[:, :].unsqueeze(1).broadcast_to([P, H, P]), ALU.add).then_inc(gb_pool, 1)

            @block.scalar
            def _(act):
                def take_fox(n, slot, j, t, half):
                    act.wait_ge(pj_done, 2 * n + half + 1)
                    act.wait_ge(fox_stored[half], 32 * t + 16 * j)
                    nc.scalar.activation(fst[:, half], pj[:, half], ACT.Copy).then_inc(pj_free, 1)
                    act.wait_ge(pj_free, 2 * n + half + 3)
                    act.dma_start(fox_dram[ds((2 * t + j) * P, P), HALF * half:HALF * half + HALF],
                                  fst[:, half]).then_inc(fox_stored[half], 16)

                with act.Fori(0, NT) as t:
                    n0 = 2 * t + N2
                    split_hi(act, n0 + 1, t + (N2 + 1) // 2, 0)
                    act.wait_ge(gb_loaded, 16 * t + 16)
                    act.wait_ge(o_step, 3 * t)
                    nc.scalar.activation(xsb[:, :, :], gbm[:, :, :], ACT.Exp).then_inc(eg_done, 1)
                    act.wait_ge(rb_pool, 2 * t + 2)
                    nc.scalar.activation(rbm[:, :, :], rbm[:, :, :], ACT.Exp).then_inc(decay_done, 1)
                    act.wait_ge(gb_pool, 2 * t + 2)
                    nc.scalar.activation(gbm[:, :, :], gbm[:, :, :], ACT.Exp).then_inc(decay_done, 1)
                    act.wait_ge(qg_done, 2 * t + 2)
                    for l in range(NL):
                        for g in range(2):
                            act.wait_ge(mt_mm, 2 * NL * t + 2 * l + g + 1)
                            act.wait_ge(rr_mm, 2 * NL * t + 2 * l + g - 1 if l else 2 * NL * t)
                            nc.scalar.activation(xsb[:, GRP * g:GRP * g + GRP], pa[:, g].rearrange("p (h c) -> p h c", c=P),
                                                 ACT.Copy, scale=-1.0).then_inc(mt_out, 1)
                        if l == 1:
                            take_fox(n0, 1, 0, t, 0)
                        if l == NL - 1:
                            take_fox(n0, 1, 0, t, 1)
                            split_hi(act, n0 + 2, t + (N2 + 1) // 2, 1)
                    act.wait_ge(kw_mm, 2 * t + 1)
                    nc.scalar.activation(kct[:, :, :], pc[:, 0].rearrange("p (a c) -> p a c", c=P), ACT.Copy).then_inc(kw_out, 1)
                    act.wait_ge(kw_mm, 2 * t + 2)
                    nc.scalar.activation(wu[:, :, :], pc[:, 1].rearrange("p (h d) -> p h d", d=DH), ACT.Copy).then_inc(kw_out, 1)
                    act.wait_ge(qs_mm, 2 * t + 2)
                    nc.scalar.activation(oq, pb[:, 0].rearrange("p (a c) -> p a c", c=P), ACT.Copy,
                                         scale=DH ** -0.5).then_inc(oq_out, 1)
                    take_fox(n0 + 1, 0, 1, t, 0)
                    act.wait_ge(o_step, 3 * t + 1)
                    nc.scalar.activation(osq, o_t, ACT.Square).then_inc(osq_done, 1)
                    act.wait_ge(ossq_mm, t + 1)
                    nc.scalar.activation(ors, pc[:, 0].rearrange("p (a c) -> p a c", c=P), ACT.Ln, bias=eps_t,
                                         scale=1.0 / DH).then_inc(ors_done, 1)
                    act.wait_ge(ors_done, 2 * t + 1)
                    nc.scalar.activation(ors, ors, ACT.Exp, scale=-0.5).then_inc(ors_done, 1)
                    take_fox(n0 + 1, 0, 1, t, 1)
                for half in range(2):
                    act.wait_ge(fox_stored[half], 16 * N_FOX)

            @block.vector
            def _(dve):
                nc.vector.memset(state[:, :, :], 0.0).then_inc(state_zero, 1)
                with dve.Fori(0, NT) as t:
                    n0 = 2 * t + N2
                    split_lo(dve, n0 + 1, 0)
                    k_tok = pc[:, 0].rearrange("p (h d) -> p h d", d=DH)
                    v_tok = pc[:, 1].rearrange("p (h d) -> p h d", d=DH)
                    dve.wait_ge(kv_turned, 2 * t + 1)
                    nc.vector.tensor_tensor(kbg[:, :, :], k_tok, per_head(bg_tok, t).broadcast_to([P, H, DH]),
                                            ALU.mult).then_inc(kv_scaled, 1)
                    nc.vector.tensor_tensor(ktail[:, :, :], k_tok, per_head(kt_tok, t).broadcast_to([P, H, DH]),
                                            ALU.mult).then_inc(kv_scaled, 1)
                    dve.wait_ge(kv_turned, 2 * t + 2)
                    nc.vector.tensor_tensor(vb[:, :, :], v_tok, per_head(b_tok, t).broadcast_to([P, H, DH]),
                                            ALU.mult).then_inc(kv_scaled, 1)
                    dve.wait_ge(decay_done, 2 * t + 1)
                    for g in range(2):
                        hs = slice(GRP * g, GRP * g + GRP)
                        dve.wait_ge(kk_mm, 2 * t + g + 1)
                        nc.vector.tensor_tensor(rbm[:, hs], pa[:, g].rearrange("p (h c) -> p h c", c=P), rbm[:, hs],
                                                ALU.mult).then_inc(m_done, 1)
                        dve.wait_ge(m_done, 2 * t + g + 1)
                        r0 = 14 * t + 2 * g
                        nc.vector.tensor_tensor(rt[:, hs], rbm[:, hs], neg_m1[:, :].unsqueeze(1).broadcast_to([P, GRP, P]),
                                                ALU.mult).then_inc(r_step, 1)
                        dve.wait_ge(r_step, r0 + 1)
                        nc.vector.tensor_tensor(rt[:, hs], rt[:, hs], ident[:, :].unsqueeze(1).broadcast_to([P, GRP, P]),
                                                ALU.add).then_inc(r_step, 1)
                        dve.wait_ge(r_step, r0 + 2)
                        nc.vector.transpose(tt[:, hs], rt[:, hs]).then_inc(t_done, 1)
                    dve.wait_ge(eg_done, t + 1)
                    dve.wait_ge(tile_copied, 3 * t + 3)
                    for parity in range(2):
                        rows = slice(DH * parity, DH * parity + DH)
                        nc.vector.tensor_tensor(qg[rows], qfix[rows],
                                                xsb[rows, GRP * parity:GRP * parity + GRP],
                                                ALU.mult).then_inc(qg_done, 1)
                    dve.wait_ge(decay_done, 2 * t + 2)
                    for g in range(2):
                        hs = slice(GRP * g, GRP * g + GRP)
                        dve.wait_ge(qk_mm, 2 * t + g + 1)
                        nc.vector.tensor_tensor(gbm[:, hs], pb[:, g].rearrange("p (h c) -> p h c", c=P), gbm[:, hs],
                                                ALU.mult).then_inc(a_done, 1)
                    for l in range(NL):
                        for g in range(2):
                            hs = slice(GRP * g, GRP * g + GRP)
                            dve.wait_ge(rr_mm, 2 * NL * t + 2 * l + g + 1)
                            alone(dve)
                            nc.vector.copy_predicated(rt[:, hs], lev[:, l].unsqueeze(1).broadcast_to([P, GRP, P]),
                                                      pb[:, g].rearrange("p (h c) -> p h c", c=P)).then_inc(r_step, 1)
                            if l < NL - 1:
                                dve.wait_ge(r_step, 14 * t + 5 + 2 * l + g)
                                nc.vector.transpose(tt[:, hs], rt[:, hs]).then_inc(t_done, 1)
                    split_lo(dve, n0 + 2, 1)
                    dve.wait_ge(kw_out, 2 * t + 2)
                    for c in range(2):
                        rows = slice(DH * c, DH * c + DH)
                        dve.wait_ge(ks_mm, 2 * t + c + 1)
                        nc.vector.tensor_tensor(u[rows], wu[rows], pa[rows, 0].rearrange("p (h d) -> p h d", d=DH),
                                                ALU.subtract).then_inc(u_done, 1)
                        dve.wait_ge(qs_mm, 2 * t + c + 1)
                        for parity in range(2):
                            rows = slice(DH * parity, DH * parity + DH)
                            block_ = state[rows, :, DH * parity:DH * parity + DH]
                            decay = gl[rows, c, ds(t * H + parity, PAIRS, 2)].unsqueeze(2).broadcast_to([DH, PAIRS, DH])
                            nc.vector.tensor_tensor(block_, block_, decay, ALU.mult).then_inc(s_step, 1)
                        dve.wait_ge(su_mm, 2 * t + c + 1)
                        dve.wait_ge(s_step, 8 * t + 4 * c + 2)
                        for parity in range(2):
                            rows = slice(DH * parity, DH * parity + DH)
                            block_ = state[rows, :, DH * parity:DH * parity + DH]
                            new = pa[rows, 1].rearrange("p (a e) -> p a e", e=P)[:, :, DH * parity:DH * parity + DH]
                            nc.vector.tensor_tensor(block_, block_, new, ALU.add).then_inc(s_step, 1)
                    dve.wait_ge(au_mm, t + 1)
                    dve.wait_ge(oq_out, t + 1)
                    nc.vector.scalar_tensor_tensor(o_t, pb[:, 1].rearrange("p (a c) -> p a c", c=P), DH ** -0.5, oq,
                                                   ALU.mult, ALU.add).then_inc(o_step, 1)
                    dve.wait_ge(ors_done, 2 * t + 2)
                    nc.vector.tensor_tensor(o_t, o_t, ors, ALU.mult).then_inc(o_step, 1)
                    dve.wait_ge(o_step, 3 * t + 2)
                    z_t = zg[:, :, ds(t * P, P)]
                    nc.vector.tensor_tensor(z_t, o_t, z_t, ALU.mult).then_inc(o_step, 1)

            @block.tensor
            def _(pe):
                pe.wait_ge(state_zero, 1)
                with pe.Fori(0, NT) as t:
                    n0 = 2 * t + N2
                    done = [0]

                    def fill(count):
                        for _ in range(count):
                            tile, rest = divmod(done[0], 2 * KT)
                            project(pe, n0 + tile, 1 - tile, rest // KT, rest % KT)
                            done[0] += 1

                    pe.wait_ge(tile_copied, 3 * t + 1)
                    pe.wait_ge(ors_done, 2 * t)
                    for p in range(PAIRS):
                        last = nc.tensor.transpose(pc[:, 0, P * p:P * p + P], kfix[:, p], ident[:, :])
                    last.then_inc(kv_turned, 1)
                    pe.wait_ge(tile_copied, 3 * t + 2)
                    for p in range(PAIRS):
                        last = nc.tensor.transpose(pc[:, 1, P * p:P * p + P], vfix[:, p], ident[:, :])
                    last.then_inc(kv_turned, 1)
                    fill(2)
                    pe.wait_ge(s_step, 8 * t)
                    pe.wait_ge(o_step, 3 * t)
                    for p in range(PAIRS):
                        for g in range(2):
                            rows = slice(DH * g, DH * g + DH)
                            last = nc.tensor.matmul(pa[:, g, P * p:P * p + P], kfix[rows, p], kfix[rows, p],
                                                    start=True, stop=True)
                            if p == PAIRS - 1:
                                last.then_inc(kk_mm, 1)
                    pe.wait_ge(tile_copied, 3 * t + 3)
                    for p in range(PAIRS):
                        for g in range(2):
                            rows = slice(DH * g, DH * g + DH)
                            last = nc.tensor.matmul(pb[:, g, P * p:P * p + P], kfix[rows, p], qfix[rows, p],
                                                    start=True, stop=True)
                            if p == PAIRS - 1:
                                last.then_inc(qk_mm, 1)
                    fill(4)
                    pe.wait_ge(a_done, 2 * t + 2)
                    for l in range(NL):
                        for g in range(2):
                            pe.wait_ge(t_done, 2 * NL * t + 2 * l + g + 1)
                            for h in range(GRP * g, GRP * g + GRP):
                                last = nc.tensor.matmul(pa[:, g, P * (h - GRP * g):P * (h - GRP * g) + P], rbm[:, h],
                                                        tt[:, h], start=True, stop=True)
                            last.then_inc(mt_mm, 1)
                        fill(1)
                        for g in range(2):
                            pe.wait_ge(mt_out, 2 * NL * t + 2 * l + g + 1)
                            for h in range(GRP * g, GRP * g + GRP):
                                last = nc.tensor.matmul(pb[:, g, P * (h - GRP * g):P * (h - GRP * g) + P], xsb[:, h],
                                                        rt[:, h], start=True, stop=True)
                            last.then_inc(rr_mm, 1)
                        fill(2)
                    pe.wait_ge(kv_scaled, 3 * t + 3)
                    pe.wait_ge(r_step, 14 * t + 14)
                    for h in range(H):
                        rows = slice(DH * (h % 2), DH * (h % 2) + DH)
                        last = nc.tensor.matmul(pc[rows, 0, P * (h // 2):P * (h // 2) + P], kbg[:, h], rt[:, place(h)],
                                                start=True, stop=True)
                    last.then_inc(kw_mm, 1)
                    for h in range(H):
                        last = nc.tensor.matmul(pc[:, 1, DH * h:DH * h + DH], rt[:, place(h)], vb[:, h], start=True, stop=True)
                    last.then_inc(kw_mm, 1)
                    fill(2)
                    for c in range(2):
                        rows = slice(DH * c, DH * c + DH)
                        pe.wait_ge(kw_out, 2 * t + 2)
                        pe.wait_ge(s_step, 8 * t + 4 * c)
                        for p in range(PAIRS):
                            last = nc.tensor.matmul(pa[rows, 0, P * p:P * p + P], kct[:, p, DH * c:DH * c + DH],
                                                    state[:, p], start=True, stop=True)
                        last.then_inc(ks_mm, 1)
                        pe.wait_ge(qg_done, 2 * t + 2)
                        for p in range(PAIRS):
                            last = nc.tensor.matmul(pb[:, 0, P * p + DH * c:P * p + DH * c + DH], state[:, p],
                                                    qg[:, p, DH * c:DH * c + DH], start=True, stop=True)
                        last.then_inc(qs_mm, 1)
                        fill(1)
                        pe.wait_ge(u_done, 2 * t + c + 1)
                        for p in range(PAIRS):
                            last = nc.tensor.matmul(pa[:, 1, P * p:P * p + P],
                                                    ktail[rows, 2 * p:2 * p + 2].rearrange("p b d -> p (b d)"),
                                                    u[rows, 2 * p:2 * p + 2].rearrange("p b d -> p (b d)"),
                                                    start=True, stop=True)
                        last.then_inc(su_mm, 1)
                        fill(1)
                    for h in range(H):
                        rows = slice(DH * (h % 2), DH * (h % 2) + DH)
                        last = nc.tensor.matmul(pb[rows, 1, P * (h // 2):P * (h // 2) + P], u[:, h], gbm[:, place(h)],
                                                start=True, stop=True)
                    last.then_inc(au_mm, 1)
                    fill(2)
                    pe.wait_ge(osq_done, t + 1)
                    nc.tensor.matmul(pc[:, 0], blk_ones[:, :], osq.rearrange("p a c -> p (a c)"), start=True,
                                     stop=True).then_inc(ossq_mm, 1)
                    fill(3)
                    assert done[0] == 4 * KT

        st.close()
        if dbg == 2:
            return dump(nc, out, [zg[:, m] for m in range(PAIRS)] + [fox_dram[m * P:(m + 1) * P, :] for m in range(N_FOX)])

        outer.close()
        st = ctx.enter_context(ExitStack())
        ya_hi = sb("ya_hi", [P, PAIRS, S], F32R, where=st)
        ya_lo = sb("ya_lo", [P, PAIRS, S], F32R, where=st)
        fq = sb("fq", [P, S], where=st)
        fk = sb("fk", [P, S], where=st)
        fv = sb("fv", [P, S], where=st)
        fz = sb("fz", [P, S], where=st)
        nrm = sb("nrm", [P, S], where=st)
        sqf = sb("sqf", [P, S], where=st)
        q_st = sb("q_st", [P, S], F32R, where=st)
        k_hi = sb("k_hi", [P, S], F32R, where=st)
        k_lo = sb("k_lo", [P, S], F32R, where=st)
        v_tok = sb("v_tok", [P, NT, P], where=st)
        c_all = sb("c_all", [P, S], where=st)
        dmat = sb("dmat", [P, S], where=st)
        pbuf = sb("pbuf", [P, 2, S], where=st)
        ptb = sb("ptb", [P, NT, P], where=st)
        up_raw = sb("up_raw", [P, 2, PAIRS, P], where=st)
        up_hi = sb("up_hi", [P, 2, PAIRS, P], F32R, where=st)
        up_lo = sb("up_lo", [P, 2, PAIRS, P], F32R, where=st)
        gate = sb("gate", [P, HALF], where=st)
        mst = sb("mst", [P, HALF], where=st)
        row4 = sb("row4", [P, 2, 2], where=st)
        ngb = sb("ngb", [P, 2 * KT], where=st)
        pa_flat = pa[:, :, :].rearrange("p a s -> p (a s)")

        fox_in = {n: sem("fox_in_" + n) for n in "qkvz"}
        ya_hi_done = sem("ya_hi_done")
        ya_ready = sem("ya_ready")
        up_loaded = [sem("up_loaded0"), sem("up_loaded1")]
        up_hi_done = sem("up_hi_done")
        up_ready = sem("up_ready")
        up_done = sem("up_done")
        up_free = sem("up_free")
        gate_act = sem("gate_act")
        gate_plus = sem("gate_plus")
        m_stored = sem("m_stored")
        fsq_done = sem("fsq_done")
        fsum_mm = sem("fsum_mm")
        fnorm_act = sem("fnorm_act")
        f_normed = sem("f_normed")
        z_act = sem("z_act")
        z_step = sem("z_step")
        v_turned = sem("v_turned")
        v_out = sem("v_out")
        hi_stacked = sem("hi_stacked")
        stacked = sem("stacked")
        c_loaded = sem("c_loaded")
        d_step = sem("d_step")
        score_mm = sem("score_mm")
        score_out = sem("score_out")
        p_exp = sem("p_exp")
        p_step = sem("p_step")
        pt_mm = sem("pt_mm")
        pt_act = sem("pt_act")
        pt_dve = sem("pt_dve")
        pv_mm = sem("pv_mm")
        of_out = sem("of_out")
        y_step = sem("y_step")
        y_stored = sem("y_stored")
        N3 = N2 + N_FOX
        ITEMS = 2 * NT
        UNITS = 4
        FILL_HEAD = (2, 1, 2, 1, 2, 1, 2, 1)

        def split_up_hi(act, q, n, slot):
            act.wait_ge(up_loaded[slot], 16 * (n + 1))
            act.wait_ge(up_done, 2 * q if not isinstance(q, int) else max(2 * q - 2, 0))
            nc.scalar.activation(up_hi[:, slot], up_raw[:, slot], ACT.Copy).then_inc(up_hi_done, 1)

        def split_up_lo(dve, q, slot):
            dve.wait_ge(up_hi_done, q + 1)
            nc.vector.tensor_tensor(up_lo[:, slot], up_raw[:, slot], up_hi[:, slot].bitcast(F32),
                                    ALU.subtract).then_inc(up_ready, 1)

        def gate_exp(act, u, gate_col, psum, dst):
            act.wait_ge(pj_done, u + 1)
            alone(act)
            nc.scalar.activation(dst, psum, ACT.Exp, bias=ngb[:, ds(gate_col, 1)], scale=-1.0).then_inc(pj_free, 1)

        with nc.Block() as block:
            @block.sync
            def _(sp):
                with sp.Fori(0, PAIRS) as p:
                    n0 = 2 * p + N3
                    for j in range(2):
                        sp.wait_ge(up_ready, 2 * p)
                        sp.dma_start(up_raw[:, j], up_view[0][:, :, ds((2 * p + j) * P, P)]).then_inc(up_loaded[j], 16)
                    sp.wait_ge(stacked, 2 * p)
                    sp.dma_start(fq[:, :], fox_dram[ds(p * P, P), :]).then_inc(fox_in["q"], 16)
                    sp.wait_ge(y_step, 2 * p)
                    sp.dma_start(fk[:, :], fox_dram[ds((p + PAIRS) * P, P), :]).then_inc(fox_in["k"], 16)
                    sp.wait_ge(v_turned, 1 * p)
                    sp.dma_start(fv[:, :], fox_dram[ds((p + 2 * PAIRS) * P, P), :]).then_inc(fox_in["v"], 16)
                    sp.wait_ge(y_stored, 16 * p)
                    sp.dma_start(fz[:, :], fox_dram[ds((p + 3 * PAIRS) * P, P), :]).then_inc(fox_in["z"], 16)
                    load_w(sp, n0 + 1, COL_GATE + P + 2 * P * p, 0)
                    load_w(sp, n0 + 2, COL_GATE + 2 * P + 2 * P * p, 1)
                    sp.wait_ge(y_step, 2 * p + 2)
                    sp.dma_start(y_dram[ds(p * P, P), :], fz[:, :]).then_inc(y_stored, 16)
                sp.wait_ge(y_stored, 16 * PAIRS)

            @block.gpsimd
            def _(pool):
                pool.wait_ge(ya_ready, 1)
                with pool.Fori(0, PAIRS) as p:
                    for hh in range(2):
                        pool.dma_start(c_all[:, :], rows_dram[2, ds(2 * p + hh, 1), :].rearrange("a s -> (a s)")
                                       .partition_broadcast(P)).then_inc(c_loaded, 16)
                        pool.wait_ge(c_loaded, 32 * p + 16 * hh + 16)
                        for b in range(NT):
                            i = NT * hh + b
                            w = P * (b + 1)
                            pool.wait_ge(score_out, ITEMS * p + i)
                            c_i = c_tok.rearrange("p t h -> p (t h)")[:, ds(2 * p + hh + H * b, 1)].broadcast_to([P, w])
                            nc.gpsimd.tensor_tensor(dmat[:, 0:w], c_all[:, 0:w], c_i, ALU.subtract).then_inc(d_step, 1)
                            pool.wait_ge(d_step, 2 * ITEMS * p + 2 * i + 1)
                            alone(pool)
                            nc.gpsimd.affine_select(dmat[:, w - P:w], dmat[:, w - P:w], pattern=[[-1, P]], base=0,
                                                    channel_multiplier=1, compare_op=ALU.is_ge,
                                                    fill=-NEG).then_inc(d_step, 1)

            @block.scalar
            def _(act):
                nc.scalar.activation(ya_hi[:, :, :], zg[:, :, :], ACT.Copy).then_inc(ya_hi_done, 1)
                act.wait_ge(ya_ready, 1)
                with act.Fori(0, PAIRS) as p:
                    n0 = 2 * p + N3
                    u0 = 2 * n0

                    def sigmoid_gate(n):
                        act.wait_ge(gate_plus, UNITS * p + n + 1)
                        nc.scalar.activation(gate[:, :], gate[:, :], ACT.Ln).then_inc(gate_act, 1)
                        act.wait_ge(gate_act, 2 * UNITS * p + 2 * n + 1)
                        nc.scalar.activation(gate[:, :], gate[:, :], ACT.Exp, scale=-1.0).then_inc(gate_act, 1)

                    def exp_unit(n):
                        act.wait_ge(up_free, UNITS * p + n)
                        gate_exp(act, u0 + n, 2 * p + n // 2, pj[:, 0], gate[:, :])

                    def store_unit(n):
                        act.wait_ge(up_free, UNITS * p + n + 1)
                        act.dma_start(m_dram[ds((2 * p + n // 2) * P, P), HALF * (n % 2):HALF * (n % 2) + HALF],
                                      mst[:, :]).then_inc(m_stored, 16)

                    def squares(n, src):
                        act.wait_ge(fsum_mm, 3 * p + n)
                        nc.scalar.activation(sqf[:, :], src[:, :], ACT.Square).then_inc(fsq_done, 1)

                    def norms(n):
                        act.wait_ge(fsum_mm, 3 * p + n + 1)
                        nc.scalar.activation(nrm[:, :], pa_flat, ACT.Ln, bias=eps_t, scale=1.0 / DH).then_inc(fnorm_act, 1)
                        act.wait_ge(fnorm_act, 6 * p + 2 * n + 1)
                        nc.scalar.activation(nrm[:, :], nrm[:, :], ACT.Exp, scale=-0.5).then_inc(fnorm_act, 1)

                    def stack(hh):
                        rows = slice(DH * hh, DH * hh + DH)
                        nc.scalar.activation(q_st[rows], fq[rows], ACT.Copy).then_inc(hi_stacked, 1)
                        for half in (hh, 1 - hh):
                            nc.scalar.activation(k_hi[DH * half:DH * half + DH], fk[rows], ACT.Copy).then_inc(hi_stacked, 1)

                    def take_turned(i):
                        w = min(i % NT + 1, 4)
                        act.wait_ge(pt_mm, ITEMS * p + i + 1)
                        act.wait_ge(pv_mm, ITEMS * p + i)
                        nc.scalar.activation(ptb[:, 0:w], pb[:, 0, 0:P * w].rearrange("p (n c) -> p n c", c=P),
                                             ACT.Copy).then_inc(pt_act, 1)

                    def take_out(i):
                        hh, b = divmod(i, NT)
                        rows = slice(DH * hh, DH * hh + DH)
                        act.wait_ge(pv_mm, ITEMS * p + i + 1)
                        nc.scalar.activation(fk[rows, P * b:P * b + P], pc[rows, i % 2, 0:P], ACT.Copy).then_inc(of_out, 1)

                    split_hi(act, n0 + 1, p + (N3 + 1) // 2, 0)
                    for j in range(2):
                        split_up_hi(act, 2 * p, p, j)
                    act.wait_ge(fox_in["q"], 16 * p + 16)
                    squares(0, fq)
                    norms(0)
                    act.wait_ge(fox_in["k"], 16 * p + 16)
                    squares(1, fk)
                    act.wait_ge(f_normed, 2 * p + 1)
                    norms(1)
                    for b in range(2):
                        act.wait_ge(v_turned, p + 1)
                        nc.scalar.activation(v_tok[:, 4 * b:4 * b + 4], pb[:, b].rearrange("p (n c) -> p n c", c=P),
                                             ACT.Copy).then_inc(v_out, 1)
                    exp_unit(0)
                    sigmoid_gate(0)
                    store_unit(0)
                    act.wait_ge(f_normed, 2 * p + 2)
                    stack(0)
                    act.wait_ge(fox_in["z"], 16 * p + 16)
                    nc.scalar.activation(sqf[:, :], fz[:, :], ACT.Exp, scale=-1.0).then_inc(z_act, 1)
                    act.wait_ge(z_step, 2 * p + 1)
                    nc.scalar.activation(sqf[:, :], sqf[:, :], ACT.Ln).then_inc(z_act, 1)
                    act.wait_ge(z_act, 3 * p + 2)
                    nc.scalar.activation(sqf[:, :], sqf[:, :], ACT.Exp, scale=-1.0).then_inc(z_act, 1)
                    for i in range(ITEMS):
                        hh, b = divmod(i, NT)
                        w = P * (b + 1)
                        if i:
                            take_turned(i - 1)
                        act.wait_ge(score_out, ITEMS * p + i + 1)
                        nc.scalar.activation(pbuf[:, i % 2, 0:w], pbuf[:, i % 2, 0:w], ACT.Exp, bias=row4[:, i % 2, 0:1],
                                             scale=-1.0, accum_out=row4[:, i % 2, 1:2]).then_inc(p_exp, 1)
                        if i == NT - 1:
                            act.wait_ge(stacked, 2 * p + 1)
                            act.wait_ge(score_mm, ITEMS * p + NT)
                            stack(1)
                        if i:
                            take_out(i - 1)
                        if i == 4:
                            exp_unit(1)
                            sigmoid_gate(1)
                        if i == 7:
                            store_unit(1)
                        if i == 9:
                            exp_unit(2)
                            sigmoid_gate(2)
                            split_hi(act, n0 + 2, p + (N3 + 1) // 2, 1)
                        if i == 12:
                            store_unit(2)
                    take_turned(ITEMS - 1)
                    take_out(ITEMS - 1)
                    act.wait_ge(of_out, ITEMS * p + ITEMS)
                    squares(2, fk)
                    norms(2)
                    exp_unit(3)
                    sigmoid_gate(3)
                    store_unit(3)
                act.wait_ge(m_stored, 16 * UNITS * PAIRS)

            @block.vector
            def _(dve):
                dve.wait_ge(ya_hi_done, 1)
                nc.vector.tensor_tensor(ya_lo[:, :, :], zg[:, :, :], ya_hi[:, :, :].bitcast(F32),
                                        ALU.subtract).then_inc(ya_ready, 1)
                dve.wait_ge(ya_ready, 1)
                nc.vector.tensor_scalar(ngb[:, :], cst[:, 64:64 + 2 * KT], -1.0, None, ALU.mult)
                with dve.Fori(0, PAIRS) as p:
                    n0 = 2 * p + N3
                    u0 = 2 * n0

                    def plus_unit(n):
                        dve.wait_ge(pj_free, u0 + n + 3)
                        nc.vector.tensor_scalar(gate[:, :], gate[:, :], LN_MAX, 1.0, ALU.min, ALU.add).then_inc(gate_plus, 1)

                    def gated_unit(n):
                        dve.wait_ge(gate_act, 2 * UNITS * p + 2 * n + 2)
                        dve.wait_ge(up_done, UNITS * p + n + 1)
                        dve.wait_ge(m_stored, 16 * UNITS * p + 16 * n)
                        nc.vector.tensor_tensor(mst[:, :], pj[:, 1], gate[:, :], ALU.mult).then_inc(up_free, 1)

                    def stack(hh):
                        rows = slice(DH * hh, DH * hh + DH)
                        other = slice(DH * (1 - hh), DH * (1 - hh) + DH)
                        h0 = 6 * p + 3 * hh
                        dve.wait_ge(hi_stacked, h0 + 1)
                        nc.vector.tensor_tensor(q_st[other], fq[rows], q_st[rows].bitcast(F32), ALU.subtract)
                        dve.wait_ge(hi_stacked, h0 + 2)
                        nc.vector.tensor_tensor(k_lo[rows], fk[rows], k_hi[rows].bitcast(F32), ALU.subtract)
                        nc.vector.tensor_tensor(k_lo[other], fk[rows], k_hi[rows].bitcast(F32),
                                                ALU.subtract).then_inc(stacked, 1)

                    def take_turned(i):
                        b = i % NT
                        if b < 4:
                            return
                        dve.wait_ge(pt_mm, ITEMS * p + i + 1)
                        dve.wait_ge(pv_mm, ITEMS * p + i)
                        nc.vector.tensor_copy(ptb[:, 4:b + 1], pb[:, 1, 0:P * (b - 3)].rearrange("p (n c) -> p n c", c=P)
                                              ).then_inc(pt_dve, 1)

                    split_lo(dve, n0 + 1, 0)
                    for j in range(2):
                        split_up_lo(dve, 2 * p + j, j)
                    for n, (t, name) in enumerate(((fq, "q"), (fk, "k"))):
                        dve.wait_ge(fnorm_act, 6 * p + 2 * n + 2)
                        nc.vector.scalar_tensor_tensor(t[:, :], t[:, :], fox_nw[name], nrm[:, :], ALU.mult,
                                                       ALU.mult).then_inc(f_normed, 1)
                    plus_unit(0)
                    gated_unit(0)
                    dve.wait_ge(f_normed, 2 * p + 2)
                    stack(0)
                    dve.wait_ge(z_act, 3 * p + 1)
                    nc.vector.tensor_scalar(sqf[:, :], sqf[:, :], LN_MAX, 1.0, ALU.min, ALU.add).then_inc(z_step, 1)
                    for i in range(ITEMS):
                        hh, b = divmod(i, NT)
                        w = P * (b + 1)
                        dve.wait_ge(score_mm, ITEMS * p + i + 1)
                        dve.wait_ge(d_step, 2 * ITEMS * p + 2 * i + 2)
                        dve.wait_ge(pt_mm, ITEMS * p + max(i - 1, 0))
                        alone(dve)
                        nc.vector.tensor_tensor_reduce(pbuf[:, i % 2, 0:w], dmat[:, 0:w], pa_flat[:, 0:w], 1.0, 3e38,
                                                       ALU.add, ALU.min, row4[:, i % 2, 0:1]).then_inc(score_out, 1)
                        if i:
                            take_turned(i - 1)
                        dve.wait_ge(p_exp, ITEMS * p + i + 1)
                        nc.vector.reciprocal(row4[:, i % 2, 1:2], row4[:, i % 2, 1:2]).then_inc(p_step, 1)
                        dve.wait_ge(p_step, 2 * ITEMS * p + 2 * i + 1)
                        nc.vector.tensor_scalar(pbuf[:, i % 2, 0:w], pbuf[:, i % 2, 0:w], row4[:, i % 2, 1:2], None,
                                                ALU.mult).then_inc(p_step, 1)
                        if i == 0:
                            dve.wait_ge(z_act, 3 * p + 3)
                            nc.vector.scalar_tensor_tensor(fz[:, :], fz[:, :], fox_nw["o"], sqf[:, :], ALU.mult,
                                                           ALU.mult).then_inc(z_step, 1)
                        if i == NT - 1:
                            stack(1)
                        if i == 4:
                            plus_unit(1)
                        if i == 7:
                            gated_unit(1)
                        if i == 9:
                            plus_unit(2)
                            split_lo(dve, n0 + 2, 1)
                        if i == 12:
                            gated_unit(2)
                    take_turned(ITEMS - 1)
                    dve.wait_ge(fnorm_act, 6 * p + 6)
                    nc.vector.tensor_tensor(nrm[:, :], fk[:, :], nrm[:, :], ALU.mult).then_inc(y_step, 1)
                    dve.wait_ge(y_step, 2 * p + 1)
                    nc.vector.tensor_tensor(fz[:, :], fz[:, :], nrm[:, :], ALU.mult).then_inc(y_step, 1)
                    plus_unit(3)
                    gated_unit(3)

            @block.tensor
            def _(pe):
                pe.wait_ge(ya_ready, 1)
                with pe.Fori(0, PAIRS) as p:
                    n0 = 2 * p + N3
                    done = [0]

                    def fill(count):
                        for _ in range(count):
                            unit, k = divmod(done[0], KT + PAIRS)
                            tile, half = divmod(unit, 2)
                            if k < KT:
                                project(pe, n0 + tile, 1 - tile, half, k, banks=1)
                            else:
                                project_up(pe, 2 * p + tile, tile, half, k - KT, ya_hi, ya_lo, pj[:, 1],
                                           up_hi, up_lo)
                            done[0] += 1

                    def head_sums(n):
                        pe.wait_ge(fsq_done, 3 * p + n + 1)
                        for half in range(2):
                            last = nc.tensor.matmul(pa[:, half], blk_ones[:, :], sqf[:, HALF * half:HALF * half + HALF],
                                                    start=True, stop=True)
                        last.then_inc(fsum_mm, 1)

                    def turn(i):
                        pe.wait_ge(p_step, 2 * ITEMS * p + 2 * i + 2)
                        for b in range(i % NT + 1):
                            last = nc.tensor.transpose(pb[:, b // 4, P * (b % 4):P * (b % 4) + P],
                                                       pbuf[:, i % 2, P * b:P * b + P], ident[:, :])
                        last.then_inc(pt_mm, 1)

                    def values(i):
                        hh, b = divmod(i, NT)
                        rows = slice(DH * hh, DH * hh + DH)
                        pe.wait_ge(pt_act, ITEMS * p + i + 1)
                        if b >= 4:
                            pe.wait_ge(pt_dve, NT * p + 4 * hh + b - 3)
                        pe.wait_ge(of_out, ITEMS * p + max(i - 1, 0))
                        for j in range(b + 1):
                            last = nc.tensor.matmul(pc[rows, i % 2, 0:P], v_tok[:, j, rows], ptb[:, j],
                                                    start=(j == 0), stop=(j == b))
                        last.then_inc(pv_mm, 1)

                    fill(4)
                    head_sums(0)
                    fill(2)
                    pe.wait_ge(fnorm_act, 6 * p + 1)
                    head_sums(1)
                    fill(2)
                    pe.wait_ge(fox_in["v"], 16 * p + 16)
                    for t in range(NT):
                        last = nc.tensor.transpose(pb[:, t // 4, P * (t % 4):P * (t % 4) + P], fv[:, P * t:P * t + P],
                                                   ident[:, :])
                    last.then_inc(v_turned, 1)
                    fill(6)
                    pe.wait_ge(fnorm_act, 6 * p + 3)
                    pe.wait_ge(v_out, 2 * p + 2)
                    for i in range(ITEMS):
                        hh, b = divmod(i, NT)
                        if i == NT:
                            fill(4)
                        pe.wait_ge(stacked, 2 * p + hh + 1)
                        pe.wait_ge(hi_stacked, 6 * p + 3 * hh + 3)
                        pe.wait_ge(score_out, ITEMS * p + i)
                        w = P * (b + 1)
                        for lo in range(0, w, HALF):
                            cols = slice(lo, min(w, lo + HALF))
                            nc.tensor.matmul(pa_flat[:, cols], q_st[:, P * b:P * b + P], k_hi[:, cols], start=True, stop=False)
                            last = nc.tensor.matmul(pa_flat[:, cols], q_st[:, P * b:P * b + P], k_lo[:, cols],
                                                    start=False, stop=True)
                        last.then_inc(score_mm, 1)
                        fill(FILL_HEAD[b])
                        if i:
                            turn(i - 1)
                            values(i - 1)
                    turn(ITEMS - 1)
                    fill(1)
                    values(ITEMS - 1)
                    fill(1)
                    pe.wait_ge(score_out, ITEMS * p + ITEMS)
                    head_sums(2)
                    fill(4)
                    pe.wait_ge(fnorm_act, 6 * p + 5)
                    assert done[0] == UNITS * (KT + PAIRS)

        st.close()
        if dbg == 3:
            return dump(nc, out, [y_dram[m * P:(m + 1) * P, :] for m in range(PAIRS)] + [m_dram[m * P:(m + 1) * P, :] for m in range(KT)])

        merged = sb("merged", [P, KT, S])
        st = ctx.enter_context(ExitStack())
        yb = sb("yb", [P, PAIRS, S], where=st)
        yb_hi = sb("yb_hi", [P, PAIRS, S], F32R, where=st)
        yb_lo = sb("yb_lo", [P, PAIRS, S], F32R, where=st)
        up_raw = sb("up_raw_b", [P, 2, PAIRS, P], where=st)
        up_hi = sb("up_hi_b", [P, 2, PAIRS, P], F32R, where=st)
        up_lo = sb("up_lo_b", [P, 2, PAIRS, P], F32R, where=st)
        ma = sb("ma", [P, 2, S], where=st)
        gates = sb("gates", [P, 2, HALF], where=st)
        ngb = sb("ngb_b", [P, 2 * KT], where=st)

        yb_loaded = sem("yb_loaded")
        yb_hi_done = sem("yb_hi_done")
        yb_ready = sem("yb_ready")
        ngb_done = sem("ngb_done")
        upb_loaded = [sem("upb_loaded0"), sem("upb_loaded1")]
        ma_loaded = [sem("ma_loaded0"), sem("ma_loaded1")]
        gate2_act = sem("gate2_act")
        gate2_plus = sem("gate2_plus")
        up2_read = sem("up2_read")
        merge_done = sem("merge_done")
        N4 = N3 + KT
        NTILES = N4 + KT
        UP0 = 2 * UNITS * PAIRS // 2

        with nc.Block() as block:
            @block.sync
            def _(sp):
                sp.dma_start(yb[:, :, :], y_dram.rearrange("(k p) s -> p k s", p=P)).then_inc(yb_loaded, 16)

                def step(i, weights):
                    for j in range(2):
                        sp.wait_ge(up_ready, 2 * i + 2 * PAIRS)
                        sp.dma_start(up_raw[:, j], up_view[1][:, :, ds((2 * i + j) * P, P)]).then_inc(upb_loaded[j], 16)
                        sp.wait_ge(merge_done, 4 * i)
                        sp.dma_start(ma[:, j], m_dram[ds((2 * i + j) * P, P), :]).then_inc(ma_loaded[j], 16)
                        if weights > j:
                            load_w(sp, N4 + 1 + 2 * i + j, COL_GATE + (KT + 1 + j) * P + 2 * P * i, j)

                with sp.Fori(0, KT // 2 - 1) as i:
                    step(i, 2)
                step(KT // 2 - 1, 1)

            @block.scalar
            def _(act):
                act.wait_ge(yb_loaded, 16)
                nc.scalar.activation(yb_hi[:, :, :], yb[:, :, :], ACT.Copy).then_inc(yb_hi_done, 1)
                act.wait_ge(ngb_done, 1)

                def step(i, more):
                    for j in range(2):
                        act.wait_ge(upb_loaded[j], 16 * i + 16)
                        act.wait_ge(up_done, 4 * i + UP0)
                        nc.scalar.activation(up_hi[:, j], up_raw[:, j], ACT.Copy).then_inc(up_hi_done, 1)
                    for j in range(2):
                        n = 2 * i + j + N4
                        if more > j:
                            split_hi(act, n + 1, i + (N4 + 1) // 2, j)
                        for half in range(2):
                            q = 4 * i + 2 * j + half
                            act.wait_ge(up2_read, q - 1 if j or half else 4 * i)
                            act.wait_ge(pj_done, 2 * n + half + 1)
                            alone(act)
                            nc.scalar.activation(gates[:, half], pj[:, half], ACT.Exp, bias=ngb[:, ds(2 * i + j + KT, 1)],
                                                 scale=-1.0).then_inc(pj_free, 1)
                            act.wait_ge(gate2_plus, q + 1)
                            nc.scalar.activation(gates[:, half], gates[:, half], ACT.Ln).then_inc(gate2_act, 1)
                            act.wait_ge(gate2_act, 2 * q + 1)
                            nc.scalar.activation(gates[:, half], gates[:, half], ACT.Exp, scale=-1.0).then_inc(gate2_act, 1)

                with act.Fori(0, KT // 2 - 1) as i:
                    step(i, 2)
                step(KT // 2 - 1, 1)

            @block.vector
            def _(dve):
                nc.vector.tensor_scalar(ngb[:, :], cst[:, 64:64 + 2 * KT], -1.0, None, ALU.mult).then_inc(ngb_done, 1)
                dve.wait_ge(yb_hi_done, 1)
                nc.vector.tensor_tensor(yb_lo[:, :, :], yb[:, :, :], yb_hi[:, :, :].bitcast(F32),
                                        ALU.subtract).then_inc(yb_ready, 1)

                def step(i, more):
                    for j in range(2):
                        dve.wait_ge(up_hi_done, 2 * i + j + 1 + 2 * PAIRS)
                        nc.vector.tensor_tensor(up_lo[:, j], up_raw[:, j], up_hi[:, j].bitcast(F32),
                                                ALU.subtract).then_inc(up_ready, 1)
                    for j in range(2):
                        n = 2 * i + j + N4
                        if more > j:
                            split_lo(dve, n + 1, j)
                        for half in range(2):
                            q = 4 * i + 2 * j + half
                            dve.wait_ge(pj_free, 2 * n + half + 3)
                            nc.vector.tensor_scalar(gates[:, half], gates[:, half], LN_MAX, 1.0, ALU.min,
                                                    ALU.add).then_inc(gate2_plus, 1)
                            dve.wait_ge(gate2_act, 2 * q + 2)
                            dve.wait_ge(up_done, q + UP0 + 1)
                            nc.vector.tensor_tensor(gates[:, half], pa[:, half], gates[:, half], ALU.mult).then_inc(up_free, 1)
                            dve.wait_ge(up_free, q + UP0 + 1)
                            dve.wait_ge(ma_loaded[j], 16 * i + 16)
                            cols = slice(HALF * half, HALF * half + HALF)
                            nc.vector.tensor_tensor(merged[:, ds(2 * i + j, 1), cols].rearrange("p a s -> p (a s)"),
                                                    ma[:, j, cols], gates[:, half], ALU.add).then_inc(up2_read, 1)
                    dve.wait_ge(up2_read, 4 * i + 4)
                    dve.sem_inc(merge_done, 4)

                with dve.Fori(0, KT // 2 - 1) as i:
                    step(i, 2)
                step(KT // 2 - 1, 1)

            @block.tensor
            def _(pe):
                with pe.Fori(0, KT // 2) as i:
                    for j in range(2):
                        for half in range(2):
                            for k in range(KT):
                                project(pe, 2 * i + j + N4, 1 - j, half, k)
                            if j == 0 and half == 0:
                                pe.wait_ge(yb_ready, 1)
                            for k in range(PAIRS):
                                project_up(pe, 2 * i + j + 2 * PAIRS, j, half, k, yb_hi, yb_lo, pa[:, half], up_hi, up_lo)
        st.close()
        if dbg == 4:
            return dump(nc, out, [merged[:, m] for m in range(KT)])

        st = ctx.enter_context(ExitStack())
        o_hi = sb("o_hi", [P, KT, D], F32R, where=st)
        o_lo = sb("o_lo", [P, KT, D], F32R, where=st)
        xo = sb("xo", [P, 2, D], where=st)
        fn_bc = sb("fn_bc", [P, D], where=st)
        fstat = sb("fstat", [P, 2], where=st)
        wo_raw = w_raw[:, :, :, :].rearrange("p a k n -> p a (k n)")
        m_hi, m_lo = h_hi, h_lo
        banks = (pj, pa, pb, pc)

        wo_loaded = [sem("wo_loaded0"), sem("wo_loaded1")]
        wo_hi_done = sem("wo_hi_done")
        wo_ready = sem("wo_ready")
        xo_loaded = [sem("xo_loaded0"), sem("xo_loaded1")]
        fn_loaded = sem("fn_loaded")
        out_mm = sem("out_mm")
        sum_done = sem("sum_done")
        fsq2_done = sem("fsq2_done")
        final_done = sem("final_done")
        out_stored = [sem("out_stored0"), sem("out_stored1")]

        with nc.Block() as block:
            @block.sync
            def _(sp):
                sp.dma_start(fn_bc[:, :], final_norm_w.partition_broadcast(P)).then_inc(fn_loaded, 16)
                for k in range(KT):
                    if k >= 2:
                        sp.wait_ge(wo_ready, k - 1)
                    sp.dma_start(wo_raw[:, k % 2], w_out[0, P * k:P * k + P, :]).then_inc(wo_loaded[k % 2], 16)
                for t in range(NT):
                    if t >= 2:
                        sp.wait_ge(out_stored[t % 2], 16 * (t // 2))
                    sp.dma_start(xo[:, t % 2], x[0, P * t:P * t + P, :]).then_inc(xo_loaded[t % 2], 16)

            @block.scalar
            def _(act):
                for k in range(KT):
                    nc.scalar.activation(m_hi[:, k], merged[:, k], ACT.Copy).then_inc(wo_hi_done, 1)
                    act.wait_ge(wo_loaded[k % 2], 16 * (k // 2 + 1))
                    nc.scalar.activation(o_hi[:, k], wo_raw[:, k % 2], ACT.Copy).then_inc(wo_hi_done, 1)
                for t in range(NT):
                    s = t % 2
                    act.wait_ge(sum_done, 2 * t + 2)
                    if t:
                        act.wait_ge(fsq2_done, 3 * t)
                    else:
                        act.wait_ge(wo_ready, KT)
                    nc.scalar.activation(merged[:, 0], xo[:, s], ACT.Square,
                                         accum_out=fstat[:, s:s + 1]).then_inc(fsq2_done, 1)
                    act.wait_ge(fsq2_done, 3 * t + 1)
                    nc.scalar.activation(fstat[:, s:s + 1], fstat[:, s:s + 1], ACT.Ln, bias=eps_t,
                                         scale=1.0 / D).then_inc(fsq2_done, 1)
                    act.wait_ge(fsq2_done, 3 * t + 2)
                    nc.scalar.activation(fstat[:, s:s + 1], fstat[:, s:s + 1], ACT.Exp, scale=-0.5).then_inc(fsq2_done, 1)
                    act.wait_ge(final_done, t + 1)
                    act.dma_start(out[0, P * t:P * t + P, :], xo[:, s]).then_inc(out_stored[s], 16)
                for s in range(2):
                    act.wait_ge(out_stored[s], 16 * (NT // 2))

            @block.vector
            def _(dve):
                for k in range(KT):
                    dve.wait_ge(wo_hi_done, 2 * k + 1)
                    nc.vector.tensor_tensor(m_lo[:, k], merged[:, k], m_hi[:, k].bitcast(F32), ALU.subtract)
                    dve.wait_ge(wo_hi_done, 2 * k + 2)
                    nc.vector.tensor_tensor(o_lo[:, k], wo_raw[:, k % 2], o_hi[:, k].bitcast(F32),
                                            ALU.subtract).then_inc(wo_ready, 1)
                dve.wait_ge(fn_loaded, 16)
                for t in range(NT):
                    s = t % 2
                    dve.wait_ge(xo_loaded[s], 16 * (t // 2 + 1))
                    for half in range(2):
                        cols = slice(HALF * half, HALF * half + HALF)
                        dve.wait_ge(out_mm, 2 * t + half + 1)
                        nc.vector.tensor_tensor(xo[:, s, cols], xo[:, s, cols], banks[t % 4][:, half],
                                                ALU.add).then_inc(sum_done, 1)
                    dve.wait_ge(fsq2_done, 3 * t + 3)
                    nc.vector.scalar_tensor_tensor(xo[:, s], xo[:, s], fstat[:, s:s + 1], fn_bc[:, :], ALU.mult,
                                                   ALU.mult).then_inc(final_done, 1)

            @block.tensor
            def _(pe):
                def part(t, half, k):
                    o = banks[t % 4][:, half]
                    rows, cols = slice(P * t, P * t + P), slice(HALF * half, HALF * half + HALF)
                    nc.tensor.matmul(o, m_hi[:, k, rows], o_hi[:, k, cols], start=(k == 0), stop=False)
                    nc.tensor.matmul(o, m_hi[:, k, rows], o_lo[:, k, cols], start=False, stop=False)
                    last = nc.tensor.matmul(o, m_lo[:, k, rows], o_hi[:, k, cols], start=False, stop=(k == KT - 1))
                    if k == KT - 1:
                        last.then_inc(out_mm, 1)

                for k in range(KT):
                    pe.wait_ge(wo_ready, k + 1)
                    for t in range(4):
                        for half in range(2):
                            part(t, half, k)
                for t in range(4, NT):
                    for half in range(2):
                        pe.wait_ge(sum_done, 2 * (t - 4) + half + 1)
                        for k in range(KT):
                            part(t, half, k)


_INS = ['x', 'norm_w', 'w_in', 'gate_b', 'conv_w', 'a_log', 'dt_bias', 'gdn_norm_w', 'f_bias', 'fox_qn_w', 'fox_kn_w',
        'fox_on_w', 'w_up_gdn', 'w_up_fox', 'w_out', 'final_norm_w']


def kernel(**inputs):
    import numpy as _np
    import concourse.bacc as _bacc
    from concourse import mybir as _mybir
    from concourse.bass_utils import run_bass_kernel_spmd as _run

    nc = _bacc.Bacc("TRN2", target_bir_lowering=False, num_devices=1)
    arrays, args = {}, []
    for name in _INS:
        a = _np.ascontiguousarray(inputs[name])
        arrays[f"in_{name}"] = a
        args.append(nc.dram_tensor(f"in_{name}", a.shape, _mybir.dt.from_np(a.dtype), kind="ExternalInput").ap())
    x = arrays["in_x"]
    args.append(nc.dram_tensor("out_0", x.shape, _mybir.dt.from_np(x.dtype), kind="ExternalOutput").ap())
    program(nc, *args)
    r = _run(nc, [arrays], core_ids=[0])
    return r.results[0]["out_0"]


def dump(nc, out, aps):
    with nc.semaphore("dump") as d, nc.Block() as block:
        @block.sync
        def _(sp):
            for n, ap in enumerate(aps):
                sp.dma_start(out[n, :, 0:ap.shape[-1]], ap).then_inc(d, 16)
            sp.wait_ge(d, 16 * len(aps))
```

```python
from contextlib import ExitStack

import concourse.bass as bass
from concourse import mybir

F32 = mybir.dt.float32
F32R = mybir.dt.float32r
I32 = mybir.dt.int32
ALU = mybir.AluOpType
ACT = mybir.ActivationFunctionType
ds = bass.ds

P = 128
HALF = 512
EPS = 1e-6
NEG = -1e30
LN_MAX = 1e18
DH = 64
LEVELS = (2, 4, 8, 16, 32)


def program(nc, x, norm_w, w_in, gate_b, conv_w, a_log, dt_bias, gdn_norm_w, f_bias,
            fox_qn_w, fox_kn_w, fox_on_w, w_up_gdn, w_up_fox, w_out, final_norm_w, out):
    _, S, D = x.shape
    H = a_log.shape[1]
    KT = D // P
    NT = S // P
    PAIRS = H // 2
    CONV = conv_w.shape[1]
    QKV = conv_w.shape[2]
    HW = H * DH
    COL_Z = QKV
    COL_B = COL_Z + HW
    COL_A = COL_B + H
    COL_FOX = COL_A + H
    COL_F = COL_FOX + 4 * HW
    COL_GATE = COL_F + H
    QKV_T = QKV // P
    N_GDN = QKV_T + PAIRS
    N_FOX = 4 * PAIRS
    assert S == 2 * HALF and NT == 8 and KT == 8 and PAIRS == 4 and QKV_T == 12

    w_view = w_in[0].rearrange("(k p) n -> p k n", p=P)
    up_view = [w_up_gdn[0].rearrange("(k p) n -> p k n", p=P), w_up_fox[0].rearrange("(k p) n -> p k n", p=P)]
    rows_dram = nc.dram_tensor("rows_scratch", [3, H, S], F32, kind="Internal").ap()
    y_dram = nc.dram_tensor("y_scratch", [PAIRS * P, S], F32, kind="Internal").ap()
    m_dram = nc.dram_tensor("m_scratch", [D, S], F32, kind="Internal").ap()
    fox_dram = nc.dram_tensor("fox_scratch", [N_FOX * P, S], F32, kind="Internal").ap()

    ctx = ExitStack()
    with ctx:
        def sem(name):
            return ctx.enter_context(nc.semaphore(name))

        def sb(name, shape, dt=F32, where=ctx):
            return where.enter_context(nc.sbuf_tensor(name, shape, dt))

        pj = ctx.enter_context(nc.psum_tensor("pj", [P, 2, HALF], F32))
        pa = ctx.enter_context(nc.psum_tensor("pa", [P, 2, HALF], F32))
        pb = ctx.enter_context(nc.psum_tensor("pb", [P, 2, HALF], F32))
        pc = ctx.enter_context(nc.psum_tensor("pc", [P, 2, HALF], F32))

        h_hi = sb("h_hi", [P, KT, S], F32R)
        h_lo = sb("h_lo", [P, KT, S], F32R)
        w_raw = sb("w_raw", [P, 2, KT, P])
        w_hi = sb("w_hi", [P, 2, KT, P], F32R)
        w_lo = sb("w_lo", [P, 2, KT, P], F32R)
        ident = sb("ident", [P, P])
        blk_ones = sb("blk_ones", [P, P])
        cst = sb("cst", [P, P])
        vecs = sb("vecs", [P, 16])
        eps_t = vecs[:, 0:1]
        gdn_nw = vecs[:, 1:2]
        fox_nw = {"q": vecs[:, 2:3], "k": vecs[:, 3:4], "o": vecs[:, 4:5]}
        sgn, bias_raw, bias_s, alog_raw, coef = (vecs[:, 5 + n:6 + n] for n in range(5))
        toks = sb("toks", [P, 6, NT, H])
        lnb_tok, g_tok, c_tok, b_tok, bg_tok, kt_tok = (toks[:, n] for n in range(6))

        consts_loaded = sem("consts_loaded")
        w_loaded = [sem("w_loaded0"), sem("w_loaded1")]
        w_hi_done = sem("w_hi_done")
        w_ready = sem("w_ready")
        pj_done = sem("pj_done")
        pj_free = sem("pj_free")
        passed = sem("passed")
        SMALL_DMAS = 3

        def alone(eng):
            eng.sem_inc(passed, 1)

        def load_w(sp, m, col, slot):
            if not (isinstance(m, int) and m < 2):
                sp.wait_ge(w_ready, m - 1)
            sp.dma_start(w_raw[:, slot], w_view[:, :, ds(col, P)]).then_inc(w_loaded[slot], 16)

        def loads_of(m2, slot):
            return 16 * (m2 + 1) + (16 * (SMALL_DMAS - 1) if slot == 0 else 0)

        def split_hi(act, m, m2, slot):
            act.wait_ge(w_loaded[slot], loads_of(m2, slot))
            if not (isinstance(m, int) and m < 2):
                act.wait_ge(pj_done, 2 * (m - 1))
            nc.scalar.activation(w_hi[:, slot], w_raw[:, slot], ACT.Copy).then_inc(w_hi_done, 1)

        def split_lo(dve, m, slot):
            dve.wait_ge(w_hi_done, m + 1)
            nc.vector.tensor_tensor(w_lo[:, slot], w_raw[:, slot], w_hi[:, slot].bitcast(F32),
                                    ALU.subtract).then_inc(w_ready, 1)

        def project(pe, n, slot, half, k, banks=2):
            if k == 0:
                if half == 0:
                    pe.wait_ge(w_ready, n + 1)
                pe.wait_ge(pj_free, 2 * n + half + 3 - banks)
            o = pj[:, half * (banks - 1)]
            cols = slice(HALF * half, HALF * half + HALF)
            nc.tensor.matmul(o, w_hi[:, slot, k], h_hi[:, k, cols], start=(k == 0), stop=False)
            nc.tensor.matmul(o, w_hi[:, slot, k], h_lo[:, k, cols], start=False, stop=False)
            last = nc.tensor.matmul(o, w_lo[:, slot, k], h_hi[:, k, cols], start=False, stop=(k == KT - 1))
            if k == KT - 1:
                last.then_inc(pj_done, 1)


        def project_up(pe, q, slot, half, k, y_hi, y_lo, o, up_hi, up_lo):
            if k == 0:
                if half == 0:
                    pe.wait_ge(up_ready, q + 1)
                pe.wait_ge(up_free, 2 * q + half)
            cols = slice(HALF * half, HALF * half + HALF)
            nc.tensor.matmul(o, up_hi[:, slot, k], y_hi[:, k, cols], start=(k == 0), stop=False)
            nc.tensor.matmul(o, up_hi[:, slot, k], y_lo[:, k, cols], start=False, stop=False)
            last = nc.tensor.matmul(o, up_lo[:, slot, k], y_hi[:, k, cols], start=False, stop=(k == PAIRS - 1))
            if k == PAIRS - 1:
                last.then_inc(up_done, 1)

        mask_m = sb("mask_m", [P, P])
        mask_a = sb("mask_a", [P, P])
        neg_m1 = sb("neg_m1", [P, P])
        lev = sb("lev", [P, len(LEVELS), P], I32)
        gl = sb("gl", [P, 2, NT * H])
        outer = ctx.enter_context(ExitStack())
        qkv = sb("qkv", [P, QKV_T, S], where=outer)
        zg = sb("zg", [P, PAIRS, S], where=outer)
        st = outer.enter_context(ExitStack())
        xc = sb("xc", [P, CONV - 1 + S], where=st)
        ebuf = sb("ebuf", [P, S], where=st)
        sq = sb("sq", [P, S], where=st)
        rst = sb("rst", [P, S], where=st)
        crow = sb("crow", [P, S], where=st)
        rb_row = sb("rb_row", [P, S], where=st)
        rows_in = sb("rows_in", [P, P], where=st)
        stat = sb("stat", [P, NT], where=st)
        e_last = sb("e_last", [P, 2, P], where=st)
        xt, xs, nw_bc = qkv[:, 0:NT], qkv[:, NT:NT + 4], ebuf[:, :]
        u_row, e_row, sp_row, keep_row = (zg[:, n] for n in range(4))

        sbm = sb("sbm", [P, 2, P], where=st)
        levf = sb("levf", [P, len(LEVELS) + 1, P], where=st)

        masks = sem("masks")
        masks_done = sem("masks_done")
        small_zeroed = sem("small_zeroed")
        rows_zeroed = sem("rows_zeroed")
        x_loaded = [sem(f"x_loaded{t}") for t in range(NT)]
        nw_loaded = sem("nw_loaded")
        rstd_step = sem("rstd_step")
        xs_done = sem("xs_done")
        x_turned = sem("x_turned")
        h_hi_done = sem("h_hi_done")
        h_done = sem("h_done")
        cst_turned = sem("cst_turned")
        vec_step = sem("vec_step")
        alog_exp = sem("alog_exp")
        row_act = sem("row_act")
        row_dve = sem("row_dve")
        rows_stored = sem("rows_stored")
        tok_turned = sem("tok_turned")
        tok_dve = sem("tok_dve")
        tok_act = sem("tok_act")
        last_picked = sem("last_picked")
        conv_step = sem("conv_step")
        exp_done = sem("exp_done")
        silu_step = sem("silu_step")
        sq_done = sem("sq_done")
        ssq_done = sem("ssq_done")
        norm_act = sem("norm_act")
        qk_normed = sem("qk_normed")
        NV = 8

        with nc.Block() as block:
            @block.sync
            def _(sp):
                for t in range(NT):
                    sp.dma_start(xt[:, t], x[0, P * t:P * t + P, :]).then_inc(x_loaded[t], 16)
                sp.wait_ge(small_zeroed, 1)
                sp.dma_start(w_raw[:, 0, :, 0:H], w_view[:, :, COL_B:COL_B + H]).then_inc(w_loaded[0], 16)
                sp.dma_start(w_raw[:, 0, :, 32:32 + H], w_view[:, :, COL_A:COL_A + H]).then_inc(w_loaded[0], 16)
                sp.dma_start(w_raw[:, 0, :, 64:64 + H], w_view[:, :, COL_F:COL_F + H]).then_inc(w_loaded[0], 16)
                load_w(sp, 1, 0, 1)
                sp.wait_ge(vec_step, 1)
                for dst, src in ((gdn_nw[0:DH], gdn_norm_w), (gdn_nw[DH:P], gdn_norm_w),
                                 (fox_nw["q"][0:DH], fox_qn_w), (fox_nw["q"][DH:P], fox_qn_w),
                                 (fox_nw["k"][0:DH], fox_kn_w), (fox_nw["k"][DH:P], fox_kn_w),
                                 (fox_nw["o"][0:DH], fox_on_w), (fox_nw["o"][DH:P], fox_on_w),
                                 (bias_raw[32:32 + H], dt_bias), (bias_raw[64:64 + H], f_bias),
                                 (alog_raw[32:32 + H], a_log)):
                    sp.dma_start(dst, src[0].rearrange("(p o) -> p o", o=1)).then_inc(consts_loaded, 16)
                sp.wait_ge(rows_zeroed, 1)
                sp.dma_start(rows_in[0:CONV * QKV_T, :],
                               conv_w[0].rearrange("k (m p) -> (k m) p", p=P)).then_inc(consts_loaded, 16)
                sp.dma_start(rows_in[64:64 + 2 * KT, :],
                               gate_b[0].rearrange("(m p) -> m p", p=P)).then_inc(consts_loaded, 16)
                with sp.Fori(0, N_GDN // 2 - 1) as i:
                    for j in range(2):
                        load_w(sp, 2 * i + j + 2, (2 * i + j + 1) * P, j)
                load_w(sp, N_GDN, (N_GDN - 1) * P, 0)
                load_w(sp, N_GDN + 1, COL_FOX, 1)
                sp.wait_ge(row_dve, 6)
                for n, rows in enumerate((crow[32:32 + H], rb_row[32:32 + H], crow[64:64 + H])):
                    to = rows_dram[n].rearrange("(b a) s -> a b s", b=2) if n < 2 else rows_dram[n]
                    sp.dma_start(to, rows).then_inc(rows_stored, 16)
                sp.wait_ge(rows_stored, 48)

            @block.gpsimd
            def _(pool):
                made = [0]

                def link(ins):
                    made[0] += 1
                    ins.then_inc(masks, 1)
                    pool.wait_ge(masks, made[0])

                nc.gpsimd.memset(w_raw[:, 0], 0.0).then_inc(small_zeroed, 1)
                nc.gpsimd.memset(rows_in[:, :], 0.0).then_inc(rows_zeroed, 1)
                link(nc.gpsimd.memset(ident[:, :], 0.0))
                link(nc.gpsimd.affine_select(ident[:, :], ident[:, :], pattern=[[-1, P]], base=0,
                                             channel_multiplier=1, compare_op=ALU.not_equal, fill=1.0))
                link(nc.gpsimd.memset(mask_a[:, :], 0.0))
                link(nc.gpsimd.affine_select(mask_m[:, :], mask_a[:, :], pattern=[[1, P]], base=0,
                                             channel_multiplier=-1, compare_op=ALU.is_gt, fill=NEG))
                link(nc.gpsimd.affine_select(mask_a[:, :], mask_a[:, :], pattern=[[1, P]], base=0,
                                             channel_multiplier=-1, compare_op=ALU.is_ge, fill=NEG))
                link(nc.gpsimd.memset(mask_m[0:DH, DH:P], NEG))
                link(nc.gpsimd.memset(mask_a[0:DH, DH:P], NEG))
                link(nc.gpsimd.memset(e_last[:, :, :], 0.0))
                for c in range(2):
                    link(nc.gpsimd.affine_select(e_last[:, c], e_last[:, c], pattern=[[0, P]],
                                                 base=-(DH * c + DH - 1), channel_multiplier=1,
                                                 compare_op=ALU.not_equal, fill=1.0))

                def same_block(dst, b):
                    v = dst.rearrange("p (n b) -> p n b", b=b)
                    link(nc.gpsimd.memset(dst, 1.0))
                    link(nc.gpsimd.affine_select(v, v, pattern=[[-b, P // b], [0, b]], base=0,
                                                 channel_multiplier=1, compare_op=ALU.is_ge, fill=0.0))
                    link(nc.gpsimd.affine_select(v, v, pattern=[[b, P // b], [0, b]], base=b - 1,
                                                 channel_multiplier=-1, compare_op=ALU.is_ge, fill=0.0))

                same_block(sbm[:, 0], 1)
                for n, b in enumerate((1,) + LEVELS):
                    small, large = sbm[:, n % 2], sbm[:, (n + 1) % 2]
                    same_block(large, 2 * b)
                    link(nc.gpsimd.tensor_tensor(levf[:, n], large, small, ALU.subtract))
                    link(nc.gpsimd.affine_select(levf[:, n], levf[:, n], pattern=[[1, P]], base=0,
                                                 channel_multiplier=-1, compare_op=ALU.is_gt, fill=0.0))
                same_block(blk_ones[:, :], DH)
                link(nc.gpsimd.tensor_scalar(neg_m1[:, :], levf[:, 0], -1.0, None, ALU.mult))
                nc.gpsimd.tensor_copy(lev[:, :, :], levf[:, 1:len(LEVELS) + 1]).then_inc(masks_done, 1)

            @block.scalar
            def _(act):
                nc.scalar.preload_act_table_set("natural_log_exp_and_others")
                act.sem_inc(pj_free, 2)
                act.dma_start(nw_bc, norm_w[0, :].partition_broadcast(P)).then_inc(nw_loaded, 16)
                act.wait_ge(vec_step, 2)

                def stats(t):
                    act.wait_ge(x_loaded[t], 16)
                    if t:
                        act.wait_ge(rstd_step, 3 * t)
                    nc.scalar.activation(sq[:, :], xt[:, t], ACT.Square, accum_out=stat[:, t:t + 1]).then_inc(rstd_step, 1)
                    act.wait_ge(rstd_step, 3 * t + 1)
                    nc.scalar.activation(stat[:, t:t + 1], stat[:, t:t + 1], ACT.Ln, bias=eps_t,
                                         scale=1.0 / D).then_inc(rstd_step, 1)
                    act.wait_ge(rstd_step, 3 * t + 2)
                    nc.scalar.activation(stat[:, t:t + 1], stat[:, t:t + 1], ACT.Exp, scale=-0.5).then_inc(rstd_step, 1)

                stats(0)
                stats(1)
                for t in range(NT):
                    if t + 2 < NT:
                        stats(t + 2)
                    for b in range(2):
                        act.wait_ge(x_turned, 2 * t + b + 1)
                        nc.scalar.activation(h_hi[:, 4 * b:4 * b + 4, P * t:P * t + P],
                                             pa[:, b].rearrange("p (k c) -> p k c", c=P), ACT.Copy).then_inc(h_hi_done, 1)
                split_hi(act, 0, 0, 0)
                split_hi(act, 1, 0, 1)
                act.wait_ge(consts_loaded, 16 * 13)
                nc.scalar.activation(coef, alog_raw, ACT.Exp).then_inc(alog_exp, 1)
                act.wait_ge(vec_step, 10)
                for half in range(2):
                    act.wait_ge(pj_done, half + 1)
                    nc.scalar.activation(u_row[:, HALF * half:HALF * half + HALF], pj[:, half], ACT.Identity,
                                         bias=bias_s, scale=sgn).then_inc(pj_free, 1)
                split_hi(act, 2, 1, 0)
                act.wait_ge(pj_free, 4)
                nc.scalar.activation(e_row, u_row, ACT.Abs).then_inc(row_act, 1)
                act.wait_ge(row_act, 1)
                nc.scalar.activation(e_row, e_row, ACT.Exp, scale=-1.0).then_inc(row_act, 1)
                act.wait_ge(row_act, 2)
                nc.scalar.activation(e_row, e_row, ACT.Ln, bias=1.0).then_inc(row_act, 1)

                def sigmoid_act(n):
                    act.wait_ge(silu_step, 2 * (n - 1) + 1)
                    nc.scalar.activation(ebuf[:, :], ebuf[:, :], ACT.Ln).then_inc(exp_done, 1)
                    act.wait_ge(exp_done, 3 * (n - 1) + 2)
                    nc.scalar.activation(ebuf[:, :], ebuf[:, :], ACT.Exp, scale=-1.0).then_inc(exp_done, 1)

                def take(n, slot, m2):
                    for half in range(2):
                        act.wait_ge(pj_done, 2 * n + half + 1)
                        nc.scalar.activation(xc[:, CONV - 1 + HALF * half:CONV - 1 + HALF * half + HALF],
                                             pj[:, half], ACT.Copy).then_inc(pj_free, 1)
                    if m2 is not None:
                        split_hi(act, n + 2, m2, slot)

                def take_qkv(n, slot, m2, j=None):
                    act.wait_ge(conv_step, CONV * (n - 1))
                    take(n, slot, m2)
                    if j is not None:
                        norms(j)
                    act.wait_ge(conv_step, CONV * n)
                    act.wait_ge(silu_step, 2 * (n - 1))
                    nc.scalar.activation(ebuf[:, :], qkv[:, ds(n - 1, 1)].rearrange("p a s -> p (a s)"),
                                         ACT.Exp, scale=-1.0).then_inc(exp_done, 1)
                    sigmoid_act(n)

                def take_z(n, slot, m2, j):
                    act.wait_ge(silu_step, 2 * (n - 1))
                    take(n, slot, m2)
                    act.wait_ge(pj_free, 2 * n + 4)
                    nc.scalar.activation(ebuf[:, :], xc[:, CONV - 1:], ACT.Exp, scale=-1.0).then_inc(exp_done, 1)
                    norms(j)
                    sigmoid_act(n)

                def squares(j):
                    act.wait_ge(ssq_done, 1 * j)
                    nc.scalar.activation(sq[:, :], qkv[:, ds(j, 1)].rearrange("p a s -> p (a s)"),
                                         ACT.Square).then_inc(sq_done, 1)

                def norms(j):
                    act.wait_ge(ssq_done, j + 1)
                    act.wait_ge(qk_normed, 1 * j)
                    nc.scalar.activation(rst[:, :], pa[:, :, :].rearrange("p a s -> p (a s)"), ACT.Ln,
                                         bias=eps_t).then_inc(norm_act, 1)
                    act.wait_ge(norm_act, 2 * j + 1)
                    nc.scalar.activation(rst[:, :], rst[:, :], ACT.Exp, scale=-0.5).then_inc(norm_act, 1)

                with act.Fori(0, 2 * PAIRS // 2) as i:
                    for j in range(2):
                        take_qkv(2 * i + j + 1, 1 - j, i + j + 1)
                act.wait_ge(silu_step, 2 * 2 * PAIRS)
                with act.Fori(0, PAIRS // 2) as i:
                    for j in range(2):
                        squares(2 * i + j)
                        take_qkv(2 * i + j + 1 + 2 * PAIRS, 1 - j, i + j + 1 + PAIRS, 2 * i + j)
                act.wait_ge(tok_dve, 4)
                nc.scalar.activation(b_tok, lnb_tok, ACT.Exp).then_inc(tok_act, 1)
                nc.scalar.activation(bg_tok, bg_tok, ACT.Exp).then_inc(tok_act, 1)
                act.wait_ge(tok_dve, 6)
                nc.scalar.activation(kt_tok, kt_tok, ACT.Exp).then_inc(tok_act, 1)
                nc.scalar.activation(gl[:, :, :], pc[:, 0, 0:2 * NT * H].rearrange("p (c n) -> p c n", c=2),
                                     ACT.Exp).then_inc(tok_act, 1)

                def z_pair(i, splits):
                    for j in range(2):
                        squares(2 * i + j + PAIRS)
                        take_z(2 * i + j + 1 + 3 * PAIRS, 1 - j, i + j + 1 + PAIRS + PAIRS // 2 if j < splits else None,
                               2 * i + j + PAIRS)

                with act.Fori(0, PAIRS // 2 - 1) as i:
                    z_pair(i, 2)
                z_pair(PAIRS // 2 - 1, 1)

            @block.vector
            def _(dve):
                nc.vector.memset(vecs[:, :], 0.0).then_inc(vec_step, 1)
                dve.wait_ge(vec_step, 1)
                nc.vector.memset(eps_t, EPS).then_inc(vec_step, 1)
                nc.vector.memset(sgn, -1.0)
                nc.vector.memset(xc[:, 0:CONV - 1], 0.0).then_inc(vec_step, 1)
                dve.wait_ge(vec_step, 3)
                nc.vector.memset(sgn[32:64], 1.0).then_inc(vec_step, 1)
                nc.vector.memset(keep_row, 1.0).then_inc(vec_step, 1)
                dve.wait_ge(vec_step, 5)
                nc.vector.memset(keep_row[0:32], 0.0)
                nc.vector.memset(keep_row[32:64].rearrange("p (n c) -> p n c", c=DH)[:, :, 0:1],
                                 0.0).then_inc(vec_step, 1)
                dve.sem_inc(h_done, 2)
                dve.wait_ge(nw_loaded, 16)

                def scaled(t):
                    dve.wait_ge(rstd_step, 3 * t + 3)
                    if t >= 4:
                        dve.wait_ge(x_turned, 2 * (t - 4) + 2)
                    nc.vector.scalar_tensor_tensor(xs[:, t % 4], xt[:, t], stat[:, t:t + 1], nw_bc,
                                                   ALU.mult, ALU.mult).then_inc(xs_done, 1)

                scaled(0)
                scaled(1)
                for t in range(NT):
                    if t + 2 < NT:
                        scaled(t + 2)
                    for b in range(2):
                        cols = slice(P * t, P * t + P)
                        dve.wait_ge(h_hi_done, 2 * t + b + 1)
                        nc.vector.tensor_tensor(h_lo[:, 4 * b:4 * b + 4, cols], pa[:, b].rearrange("p (k c) -> p k c", c=P),
                                                h_hi[:, 4 * b:4 * b + 4, cols].bitcast(F32), ALU.subtract).then_inc(h_done, 1)
                split_lo(dve, 0, 0)
                split_lo(dve, 1, 1)
                dve.wait_ge(cst_turned, 1)
                nc.vector.tensor_copy(cst[:, :], pc[:, 1, 0:P]).then_inc(vec_step, 1)
                dve.wait_ge(consts_loaded, 16 * 13)
                nc.vector.tensor_tensor(bias_s, bias_raw, sgn, ALU.mult).then_inc(vec_step, 1)
                dve.wait_ge(alog_exp, 1)
                nc.vector.tensor_scalar(coef, coef, -1.0, None, ALU.mult).then_inc(vec_step, 1)
                nc.vector.tensor_scalar(fox_nw["q"], fox_nw["q"], -(DH ** -0.5), None, ALU.mult).then_inc(vec_step, 1)
                dve.wait_ge(vec_step, 10)
                split_lo(dve, 2, 0)
                dve.wait_ge(row_act, 3)
                nc.vector.scalar_tensor_tensor(sp_row, u_row, 0.0, e_row, ALU.max, ALU.add).then_inc(row_dve, 1)
                dve.wait_ge(row_dve, 1)
                nc.vector.tensor_scalar(sp_row, sp_row, coef, None, ALU.mult).then_inc(row_dve, 1)
                dve.wait_ge(row_dve, 2)
                nc.vector.tensor_tensor_scan(crow[:, :], keep_row, sp_row, 0.0, ALU.mult,
                                             ALU.add).then_inc(row_dve, 1)
                dve.wait_ge(row_dve, 3)
                nc.vector.tensor_copy(rb_row[32:64], crow[0:32]).then_inc(row_dve, 1)
                dve.wait_ge(row_dve, 4)
                nc.vector.tensor_tensor(rb_row[32:64], rb_row[32:64], crow[32:64], ALU.add).then_inc(row_dve, 2)

                def conv(n, slot, j=None):
                    dve.wait_ge(pj_free, 2 * n + 4)
                    y = qkv[:, ds(n - 1, 1)].rearrange("p a s -> p (a s)")
                    for d in range(CONV):
                        tap = cst[:, ds((CONV - 1 - d) * QKV_T + n - 1, 1)]
                        src = xc[:, CONV - 1 - d:CONV - 1 - d + S]
                        if d == 0:
                            nc.vector.tensor_scalar(y, src, tap, None, ALU.mult).then_inc(conv_step, 1)
                        else:
                            dve.wait_ge(conv_step, CONV * (n - 1) + d)
                            nc.vector.scalar_tensor_tensor(y, src, tap, y, ALU.mult, ALU.add).then_inc(conv_step, 1)
                    if j is not None:
                        normed(j)
                    sigmoid(n, lambda: split_lo(dve, n + 2, slot))
                    nc.vector.tensor_tensor(y, y, ebuf[:, :], ALU.mult).then_inc(silu_step, 1)

                def sigmoid(n, meanwhile=lambda: None):
                    dve.wait_ge(exp_done, 3 * (n - 1) + 1)
                    nc.vector.tensor_scalar(ebuf[:, :], ebuf[:, :], LN_MAX, 1.0, ALU.min, ALU.add).then_inc(silu_step, 1)
                    meanwhile()
                    dve.wait_ge(exp_done, 3 * n)

                def normed(j):
                    dve.wait_ge(norm_act, 2 * j + 2)
                    t = qkv[:, ds(j, 1)].rearrange("p a s -> p (a s)")
                    nc.vector.tensor_tensor(t, t, rst[:, :], ALU.mult).then_inc(qk_normed, 1)

                with dve.Fori(0, 2 * PAIRS // 2) as i:
                    for j in range(2):
                        conv(2 * i + j + 1, 1 - j)
                dve.wait_ge(tok_turned, 1)
                for n, row in enumerate((0, 32, 64)):
                    nc.vector.tensor_copy(toks[:, n], pb[:, :, :].rearrange("p a (t r) -> p (a t) r", r=P)
                                          [:, :, row:row + H]).then_inc(tok_dve, 1)
                dve.wait_ge(tok_dve, 3)
                nc.vector.tensor_tensor(bg_tok, lnb_tok, g_tok, ALU.add).then_inc(tok_dve, 1)
                with dve.Fori(0, PAIRS // 2) as i:
                    for j in range(2):
                        conv(2 * i + j + 1 + 2 * PAIRS, 1 - j, 2 * i + j)
                dve.wait_ge(last_picked, 1)
                for c in range(2):
                    rows = slice(DH * c, DH * c + DH)
                    nc.vector.tensor_tensor(kt_tok[rows], pc[rows, 0, NT * H * c:NT * H * (c + 1)].rearrange("p (t h) -> p t h", h=H),
                                            g_tok[rows], ALU.subtract).then_inc(tok_dve, 1)

                def z_pair(i, splits):
                    for j in range(2):
                        n = 2 * i + j + 1 + 3 * PAIRS
                        normed(2 * i + j + PAIRS)
                        sigmoid(n, (lambda: split_lo(dve, n + 2, 1 - j)) if j < splits else (lambda: None))
                        nc.vector.scalar_tensor_tensor(zg[:, ds(2 * i + j, 1)].rearrange("p a s -> p (a s)"),
                                                       xc[:, CONV - 1:], gdn_nw, ebuf[:, :],
                                                       ALU.mult, ALU.mult).then_inc(silu_step, 1)

                with dve.Fori(0, PAIRS // 2 - 1) as i:
                    z_pair(i, 2)
                z_pair(PAIRS // 2 - 1, 1)

            @block.tensor
            def _(pe):
                pe.wait_ge(masks, 2)
                for t in range(NT):
                    pe.wait_ge(xs_done, t + 1)
                    for b in range(2):
                        pe.wait_ge(h_done, 2 * t + b + 1)
                        for k in range(4):
                            last = nc.tensor.transpose(pa[:, b, k * P:(k + 1) * P],
                                                       xs[:, t % 4, (4 * b + k) * P:(4 * b + k + 1) * P], ident[:, :])
                        last.then_inc(x_turned, 1)
                pe.wait_ge(rows_zeroed, 1)
                pe.wait_ge(consts_loaded, 16 * 13)
                nc.tensor.transpose(pc[:, 1, 0:P], rows_in[:, :], ident[:, :]).then_inc(cst_turned, 1)
                pe.wait_ge(h_done, 2 * NT + 2)

                def project_tile(n, slot):
                    for half in range(2):
                        for k in range(KT):
                            project(pe, n, slot, half, k)

                def head_sums(j):
                    pe.wait_ge(masks_done, 1)
                    pe.wait_ge(sq_done, j + 1)
                    pe.wait_ge(norm_act, 2 * j)
                    for half in range(2):
                        last = nc.tensor.matmul(pa[:, half], blk_ones[:, :], sq[:, HALF * half:HALF * half + HALF],
                                                start=True, stop=True)
                    last.then_inc(ssq_done, 1)

                project_tile(0, 0)
                with pe.Fori(0, 2 * PAIRS // 2) as i:
                    for j in range(2):
                        project_tile(2 * i + j + 1, 1 - j)
                pe.wait_ge(row_dve, 6)
                for t in range(NT):
                    last = nc.tensor.transpose(pb[:, t // 4, (t % 4) * P:(t % 4 + 1) * P], crow[:, P * t:P * t + P],
                                               ident[:, :])
                last.then_inc(tok_turned, 1)
                with pe.Fori(0, PAIRS // 2) as i:
                    for j in range(2):
                        project_tile(2 * i + j + 1 + 2 * PAIRS, 1 - j)
                        head_sums(2 * i + j)
                pe.wait_ge(tok_dve, 4)
                pe.wait_ge(vec_step, 7)
                for c in range(2):
                    last = nc.tensor.matmul(pc[:, 0, NT * H * c:NT * H * (c + 1)], e_last[:, c],
                                            g_tok.rearrange("p t h -> p (t h)"), start=True, stop=True)
                last.then_inc(last_picked, 1)
                with pe.Fori(0, PAIRS // 2) as i:
                    for j in range(2):
                        project_tile(2 * i + j + 1 + 3 * PAIRS, 1 - j)
                        head_sums(2 * i + j + PAIRS)

        st.close()

        st = outer.enter_context(ExitStack())
        rbm = sb("rbm", [P, H, P], where=st)
        gbm = sb("gbm", [P, H, P], where=st)
        rt = sb("rt", [P, H, P], where=st)
        tt = sb("tt", [P, H, P], where=st)
        xsb = sb("xsb", [P, H, P], where=st)
        kfix = sb("kfix", [P, PAIRS, P], where=st)
        qfix = sb("qfix", [P, PAIRS, P], where=st)
        vfix = sb("vfix", [P, PAIRS, P], where=st)
        qg = sb("qg", [P, PAIRS, P], where=st)
        kbg = sb("kbg", [P, H, DH], where=st)
        ktail = sb("ktail", [P, H, DH], where=st)
        vb = sb("vb", [P, H, DH], where=st)
        kct = sb("kct", [P, PAIRS, P], where=st)
        wu = sb("wu", [P, H, DH], where=st)
        u = sb("u", [P, H, DH], where=st)
        state = sb("state", [P, PAIRS, P], where=st)
        fst = sb("fst", [P, 2, HALF], where=st)
        oq = xsb[:, 0:4]
        osq = xsb[:, 4:8]
        ors = xsb[:, 0:4]
        o_t = wu[:, :, :].rearrange("p (a b) d -> p a (b d)", b=2)

        rb_loaded = sem("rb_loaded")
        gb_loaded = sem("gb_loaded")
        tile_copied = sem("tile_copied")
        rb_pool = sem("rb_pool")
        gb_pool = sem("gb_pool")
        eg_done = sem("eg_done")
        decay_done = sem("decay_done")
        kv_turned = sem("kv_turned")
        kv_scaled = sem("kv_scaled")
        qg_done = sem("qg_done")
        kk_mm = sem("kk_mm")
        qk_mm = sem("qk_mm")
        m_done = sem("m_done")
        a_done = sem("a_done")
        r_step = sem("r_step")
        t_done = sem("t_done")
        mt_mm = sem("mt_mm")
        mt_out = sem("mt_out")
        rr_mm = sem("rr_mm")
        kw_mm = sem("kw_mm")
        kw_out = sem("kw_out")
        ks_mm = sem("ks_mm")
        qs_mm = sem("qs_mm")
        su_mm = sem("su_mm")
        au_mm = sem("au_mm")
        u_done = sem("u_done")
        s_step = sem("s_step")
        state_zero = sem("state_zero")
        oq_out = sem("oq_out")
        o_sum = sem("o_sum")
        o_step = sem("o_step")
        osq_done = sem("osq_done")
        ossq_mm = sem("ossq_mm")
        ors_done = sem("ors_done")
        fox_out = sem("fox_out")
        fox_stored = [sem("fox_stored0"), sem("fox_stored1")]
        NL = len(LEVELS)
        N2 = N_GDN + 1
        GRP = H // 2

        def place(h):
            return GRP * (h % 2) + h // 2

        def per_head(rows, t):
            return rows.rearrange("p t h -> p (t h)")[:, ds(t * H, H)].unsqueeze(2)

        with nc.Block() as block:
            @block.sync
            def _(sp):
                def step(t, last_col):
                    sp.wait_ge(mt_mm, 2 * NL * t)
                    sp.dma_start(rbm[:, :, :], rows_dram[1, :, ds(t * P, P)].partition_broadcast(P)).then_inc(rb_loaded, 16)
                    load_w(sp, N2 + 1 + 2 * t, COL_FOX + P + 2 * P * t, 0)
                    sp.wait_ge(au_mm, 1 * t)
                    alone(sp)
                    sp.dma_start(gbm[:, :, :], rows_dram[0, :, ds(t * P, P)].partition_broadcast(P)).then_inc(gb_loaded, 16)
                    load_w(sp, N2 + 2 + 2 * t, last_col, 1)

                with sp.Fori(0, NT - 1) as t:
                    step(t, COL_FOX + 2 * P + 2 * P * t)
                step(NT - 1, COL_GATE)

            @block.gpsimd
            def _(pool):
                def by_parity(buf):
                    return buf[:, :, :].rearrange("p (b a) c -> p b a c", b=2)

                with pool.Fori(0, NT) as t:
                    tok_by_parity = g_tok.rearrange("p t h -> p (t h)")[:, ds(t * H, H)].rearrange(
                        "p (a b) -> p b a", b=2).unsqueeze(3).broadcast_to([P, 2, GRP, P])
                    pool.wait_ge(qk_mm, 2 * t)
                    pool.wait_ge(qg_done, 2 * t)
                    for n, dst in ((1, kfix), (2, vfix), (0, qfix)):
                        nc.gpsimd.tensor_copy(dst[:, :, :], qkv[:, PAIRS * n:PAIRS * (n + 1), ds(t * P, P)]).then_inc(tile_copied, 1)
                    pool.wait_ge(rb_loaded, 16 * t + 16)
                    nc.gpsimd.tensor_tensor(by_parity(rbm), by_parity(rbm), tok_by_parity,
                                            ALU.subtract).then_inc(rb_pool, 1)
                    pool.wait_ge(rb_pool, 2 * t + 1)
                    nc.gpsimd.tensor_tensor(rbm[:, :, :], rbm[:, :, :],
                                            mask_m[:, :].unsqueeze(1).broadcast_to([P, H, P]), ALU.add).then_inc(rb_pool, 1)
                    pool.wait_ge(eg_done, t + 1)
                    alone(pool)
                    nc.gpsimd.tensor_tensor(by_parity(gbm), by_parity(gbm), tok_by_parity,
                                            ALU.subtract).then_inc(gb_pool, 1)
                    pool.wait_ge(gb_pool, 2 * t + 1)
                    nc.gpsimd.tensor_tensor(gbm[:, :, :], gbm[:, :, :],
                                            mask_a[:, :].unsqueeze(1).broadcast_to([P, H, P]), ALU.add).then_inc(gb_pool, 1)

            @block.scalar
            def _(act):
                def take_fox(n, slot, j, t, half):
                    act.wait_ge(pj_done, 2 * n + half + 1)
                    act.wait_ge(fox_stored[half], 32 * t + 16 * j)
                    nc.scalar.activation(fst[:, half], pj[:, half], ACT.Copy).then_inc(pj_free, 1)
                    act.wait_ge(pj_free, 2 * n + half + 3)
                    act.dma_start(fox_dram[ds((2 * t + j) * P, P), HALF * half:HALF * half + HALF],
                                  fst[:, half]).then_inc(fox_stored[half], 16)

                with act.Fori(0, NT) as t:
                    n0 = 2 * t + N2
                    act.wait_ge(rb_pool, 2 * t + 2)
                    nc.scalar.activation(rbm[:, :, :], rbm[:, :, :], ACT.Exp).then_inc(decay_done, 1)
                    act.wait_ge(gb_loaded, 16 * t + 16)
                    act.wait_ge(o_step, 2 * t)
                    nc.scalar.activation(xsb[:, :, :], gbm[:, :, :], ACT.Exp).then_inc(eg_done, 1)
                    split_hi(act, n0 + 1, t + (N2 + 1) // 2, 0)
                    act.wait_ge(gb_pool, 2 * t + 2)
                    nc.scalar.activation(gbm[:, :, :], gbm[:, :, :], ACT.Exp).then_inc(decay_done, 1)
                    take_fox(n0, 1, 0, t, 0)
                    act.wait_ge(qg_done, 2 * t + 2)
                    for l in range(NL):
                        for g in range(2):
                            act.wait_ge(mt_mm, 2 * NL * t + 2 * l + g + 1)
                            act.wait_ge(rr_mm, 2 * NL * t + 2 * l + g - 1 if l else 2 * NL * t)
                            nc.scalar.activation(xsb[:, GRP * g:GRP * g + GRP], pa[:, g].rearrange("p (h c) -> p h c", c=P),
                                                 ACT.Copy, scale=-1.0).then_inc(mt_out, 1)
                        if l == NL - 1:
                            take_fox(n0, 1, 0, t, 1)
                            split_hi(act, n0 + 2, t + (N2 + 1) // 2, 1)
                    act.wait_ge(kw_mm, 2 * t + 1)
                    nc.scalar.activation(kct[:, :, :], pc[:, 0].rearrange("p (a c) -> p a c", c=P), ACT.Copy).then_inc(kw_out, 1)
                    act.wait_ge(kw_mm, 2 * t + 2)
                    nc.scalar.activation(wu[:, :, :], pc[:, 1].rearrange("p (h d) -> p h d", d=DH), ACT.Copy).then_inc(kw_out, 1)
                    act.wait_ge(qs_mm, 2 * t + 2)
                    nc.scalar.activation(oq, pb[:, 0].rearrange("p (a c) -> p a c", c=P), ACT.Copy,
                                         scale=DH ** -0.5).then_inc(oq_out, 1)
                    take_fox(n0 + 1, 0, 1, t, 0)
                    act.wait_ge(o_sum, t + 1)
                    nc.scalar.activation(osq, o_t, ACT.Square).then_inc(osq_done, 1)
                    act.wait_ge(ossq_mm, t + 1)
                    nc.scalar.activation(ors, pc[:, 0].rearrange("p (a c) -> p a c", c=P), ACT.Ln, bias=eps_t,
                                         scale=1.0 / DH).then_inc(ors_done, 1)
                    act.wait_ge(ors_done, 2 * t + 1)
                    nc.scalar.activation(ors, ors, ACT.Exp, scale=-0.5).then_inc(ors_done, 1)
                    take_fox(n0 + 1, 0, 1, t, 1)
                for half in range(2):
                    act.wait_ge(fox_stored[half], 16 * N_FOX)

            @block.vector
            def _(dve):
                nc.vector.memset(state[:, :, :], 0.0).then_inc(state_zero, 1)
                with dve.Fori(0, NT) as t:
                    n0 = 2 * t + N2
                    k_tok = pc[:, 0].rearrange("p (h d) -> p h d", d=DH)
                    v_tok = pc[:, 1].rearrange("p (h d) -> p h d", d=DH)
                    dve.wait_ge(kv_turned, 2 * t + 1)
                    nc.vector.tensor_tensor(kbg[:, :, :], k_tok, per_head(bg_tok, t).broadcast_to([P, H, DH]),
                                            ALU.mult).then_inc(kv_scaled, 1)
                    nc.vector.tensor_tensor(ktail[:, :, :], k_tok, per_head(kt_tok, t).broadcast_to([P, H, DH]),
                                            ALU.mult).then_inc(kv_scaled, 1)
                    dve.wait_ge(decay_done, 2 * t + 1)
                    for g in range(2):
                        hs = slice(GRP * g, GRP * g + GRP)
                        dve.wait_ge(kk_mm, 2 * t + g + 1)
                        nc.vector.tensor_tensor(rbm[:, hs], pa[:, g].rearrange("p (h c) -> p h c", c=P), rbm[:, hs],
                                                ALU.mult).then_inc(m_done, 1)
                        dve.wait_ge(m_done, 2 * t + g + 1)
                        r0 = 14 * t + 2 * g
                        nc.vector.tensor_tensor(rt[:, hs], rbm[:, hs], neg_m1[:, :].unsqueeze(1).broadcast_to([P, GRP, P]),
                                                ALU.mult).then_inc(r_step, 1)
                        dve.wait_ge(r_step, r0 + 1)
                        nc.vector.tensor_tensor(rt[:, hs], rt[:, hs], ident[:, :].unsqueeze(1).broadcast_to([P, GRP, P]),
                                                ALU.add).then_inc(r_step, 1)
                        dve.wait_ge(r_step, r0 + 2)
                        nc.vector.transpose(tt[:, hs], rt[:, hs]).then_inc(t_done, 1)
                    dve.wait_ge(decay_done, 2 * t + 2)
                    for g in range(2):
                        hs = slice(GRP * g, GRP * g + GRP)
                        dve.wait_ge(qk_mm, 2 * t + g + 1)
                        nc.vector.tensor_tensor(gbm[:, hs], pb[:, g].rearrange("p (h c) -> p h c", c=P), gbm[:, hs],
                                                ALU.mult).then_inc(a_done, 1)
                    dve.wait_ge(eg_done, t + 1)
                    dve.wait_ge(tile_copied, 3 * t + 3)
                    for parity in range(2):
                        rows = slice(DH * parity, DH * parity + DH)
                        nc.vector.tensor_tensor(qg[rows], qfix[rows],
                                                xsb[rows, GRP * parity:GRP * parity + GRP],
                                                ALU.mult).then_inc(qg_done, 1)
                    dve.wait_ge(kv_turned, 2 * t + 2)
                    nc.vector.tensor_tensor(vb[:, :, :], v_tok, per_head(b_tok, t).broadcast_to([P, H, DH]),
                                            ALU.mult).then_inc(kv_scaled, 1)
                    split_lo(dve, n0 + 1, 0)
                    for l in range(NL):
                        for g in range(2):
                            hs = slice(GRP * g, GRP * g + GRP)
                            dve.wait_ge(rr_mm, 2 * NL * t + 2 * l + g + 1)
                            alone(dve)
                            nc.vector.copy_predicated(rt[:, hs], lev[:, l].unsqueeze(1).broadcast_to([P, GRP, P]),
                                                      pb[:, g].rearrange("p (h c) -> p h c", c=P)).then_inc(r_step, 1)
                            if l < NL - 1:
                                dve.wait_ge(r_step, 14 * t + 5 + 2 * l + g)
                                nc.vector.transpose(tt[:, hs], rt[:, hs]).then_inc(t_done, 1)
                    split_lo(dve, n0 + 2, 1)
                    dve.wait_ge(kw_out, 2 * t + 2)
                    for c in range(2):
                        rows = slice(DH * c, DH * c + DH)
                        dve.wait_ge(ks_mm, 2 * t + c + 1)
                        nc.vector.tensor_tensor(u[rows], wu[rows], pa[rows, 0].rearrange("p (h d) -> p h d", d=DH),
                                                ALU.subtract).then_inc(u_done, 1)
                        dve.wait_ge(qs_mm, 2 * t + c + 1)
                        for parity in range(2):
                            rows = slice(DH * parity, DH * parity + DH)
                            block_ = state[rows, :, DH * parity:DH * parity + DH]
                            decay = gl[rows, c, ds(t * H + parity, PAIRS, 2)].unsqueeze(2).broadcast_to([DH, PAIRS, DH])
                            nc.vector.tensor_tensor(block_, block_, decay, ALU.mult).then_inc(s_step, 1)
                        dve.wait_ge(su_mm, 2 * t + c + 1)
                        dve.wait_ge(s_step, 8 * t + 4 * c + 2)
                        for parity in range(2):
                            rows = slice(DH * parity, DH * parity + DH)
                            block_ = state[rows, :, DH * parity:DH * parity + DH]
                            new = pa[rows, 1].rearrange("p (a e) -> p a e", e=P)[:, :, DH * parity:DH * parity + DH]
                            nc.vector.tensor_tensor(block_, block_, new, ALU.add).then_inc(s_step, 1)
                    dve.wait_ge(au_mm, t + 1)
                    dve.wait_ge(oq_out, t + 1)
                    nc.vector.scalar_tensor_tensor(o_t, pb[:, 1].rearrange("p (a c) -> p a c", c=P), DH ** -0.5, oq,
                                                   ALU.mult, ALU.add).then_inc(o_sum, 1)
                    dve.wait_ge(ors_done, 2 * t + 2)
                    nc.vector.tensor_tensor(o_t, o_t, ors, ALU.mult).then_inc(o_step, 1)
                    dve.wait_ge(o_step, 2 * t + 1)
                    z_t = zg[:, :, ds(t * P, P)]
                    nc.vector.tensor_tensor(z_t, o_t, z_t, ALU.mult).then_inc(o_step, 1)

            @block.tensor
            def _(pe):
                pe.wait_ge(state_zero, 1)
                with pe.Fori(0, NT) as t:
                    n0 = 2 * t + N2
                    done = [0]

                    def fill(count):
                        for _ in range(count):
                            tile, rest = divmod(done[0], 2 * KT)
                            project(pe, n0 + tile, 1 - tile, rest // KT, rest % KT)
                            done[0] += 1

                    fill(2)
                    pe.wait_ge(tile_copied, 3 * t + 1)
                    pe.wait_ge(ors_done, 2 * t)
                    for p in range(PAIRS):
                        last = nc.tensor.transpose(pc[:, 0, P * p:P * p + P], kfix[:, p], ident[:, :])
                    last.then_inc(kv_turned, 1)
                    pe.wait_ge(tile_copied, 3 * t + 2)
                    for p in range(PAIRS):
                        last = nc.tensor.transpose(pc[:, 1, P * p:P * p + P], vfix[:, p], ident[:, :])
                    last.then_inc(kv_turned, 1)
                    pe.wait_ge(s_step, 8 * t)
                    pe.wait_ge(o_sum, t)
                    for p in range(PAIRS):
                        for g in range(2):
                            rows = slice(DH * g, DH * g + DH)
                            last = nc.tensor.matmul(pa[:, g, P * p:P * p + P], kfix[rows, p], kfix[rows, p],
                                                    start=True, stop=True)
                            if p == PAIRS - 1:
                                last.then_inc(kk_mm, 1)
                    pe.wait_ge(tile_copied, 3 * t + 3)
                    for p in range(PAIRS):
                        for g in range(2):
                            rows = slice(DH * g, DH * g + DH)
                            last = nc.tensor.matmul(pb[:, g, P * p:P * p + P], kfix[rows, p], qfix[rows, p],
                                                    start=True, stop=True)
                            if p == PAIRS - 1:
                                last.then_inc(qk_mm, 1)
                    fill(7)
                    for l in range(NL):
                        for g in range(2):
                            pe.wait_ge(t_done, 2 * NL * t + 2 * l + g + 1)
                            for h in range(GRP * g, GRP * g + GRP):
                                last = nc.tensor.matmul(pa[:, g, P * (h - GRP * g):P * (h - GRP * g) + P], rbm[:, h],
                                                        tt[:, h], start=True, stop=True)
                            last.then_inc(mt_mm, 1)
                        fill(0 if l else 2)
                        if l == 0:
                            pe.wait_ge(a_done, 2 * t + 2)
                        for g in range(2):
                            pe.wait_ge(mt_out, 2 * NL * t + 2 * l + g + 1)
                            for h in range(GRP * g, GRP * g + GRP):
                                last = nc.tensor.matmul(pb[:, g, P * (h - GRP * g):P * (h - GRP * g) + P], xsb[:, h],
                                                        rt[:, h], start=True, stop=True)
                            last.then_inc(rr_mm, 1)
                        fill(2)
                    pe.wait_ge(kv_scaled, 3 * t + 3)
                    pe.wait_ge(r_step, 14 * t + 14)
                    for h in range(H):
                        rows = slice(DH * (h % 2), DH * (h % 2) + DH)
                        last = nc.tensor.matmul(pc[rows, 0, P * (h // 2):P * (h // 2) + P], kbg[:, h], rt[:, place(h)],
                                                start=True, stop=True)
                    last.then_inc(kw_mm, 1)
                    for h in range(H):
                        last = nc.tensor.matmul(pc[:, 1, DH * h:DH * h + DH], rt[:, place(h)], vb[:, h], start=True, stop=True)
                    last.then_inc(kw_mm, 1)
                    fill(2)
                    for c in range(2):
                        rows = slice(DH * c, DH * c + DH)
                        pe.wait_ge(kw_out, 2 * t + 2)
                        pe.wait_ge(s_step, 8 * t + 4 * c)
                        for p in range(PAIRS):
                            last = nc.tensor.matmul(pa[rows, 0, P * p:P * p + P], kct[:, p, DH * c:DH * c + DH],
                                                    state[:, p], start=True, stop=True)
                        last.then_inc(ks_mm, 1)
                        pe.wait_ge(qg_done, 2 * t + 2)
                        for p in range(PAIRS):
                            last = nc.tensor.matmul(pb[:, 0, P * p + DH * c:P * p + DH * c + DH], state[:, p],
                                                    qg[:, p, DH * c:DH * c + DH], start=True, stop=True)
                        last.then_inc(qs_mm, 1)
                        fill(1)
                        pe.wait_ge(u_done, 2 * t + c + 1)
                        for p in range(PAIRS):
                            last = nc.tensor.matmul(pa[:, 1, P * p:P * p + P],
                                                    ktail[rows, 2 * p:2 * p + 2].rearrange("p b d -> p (b d)"),
                                                    u[rows, 2 * p:2 * p + 2].rearrange("p b d -> p (b d)"),
                                                    start=True, stop=True)
                        last.then_inc(su_mm, 1)
                        fill(1)
                    for h in range(H):
                        rows = slice(DH * (h % 2), DH * (h % 2) + DH)
                        last = nc.tensor.matmul(pb[rows, 1, P * (h // 2):P * (h // 2) + P], u[:, h], gbm[:, place(h)],
                                                start=True, stop=True)
                    last.then_inc(au_mm, 1)
                    fill(2)
                    pe.wait_ge(osq_done, t + 1)
                    nc.tensor.matmul(pc[:, 0], blk_ones[:, :], osq.rearrange("p a c -> p (a c)"), start=True,
                                     stop=True).then_inc(ossq_mm, 1)
                    fill(3)
                    assert done[0] == 4 * KT

        st.close()

        outer.close()
        st = ctx.enter_context(ExitStack())
        ya_hi = sb("ya_hi", [P, PAIRS, S], F32R, where=st)
        ya_lo = sb("ya_lo", [P, PAIRS, S], F32R, where=st)
        fq = sb("fq", [P, S], where=st)
        fk = sb("fk", [P, S], where=st)
        fv = sb("fv", [P, S], where=st)
        fz = sb("fz", [P, S], where=st)
        v_tok = sb("v_tok", [P, NT, P], where=st)
        c_all = sb("c_all", [P, S], where=st)
        dmat = sb("dmat", [P, 2, S], where=st)
        ptb = sb("ptb", [P, NT, P], where=st)
        sqf = sb("sqf", [P, S], where=st)
        q_st = sb("q_st", [P, S], F32R, where=st)
        k_hi = sb("k_hi", [P, S], F32R, where=st)
        k_lo = sb("k_lo", [P, S], F32R, where=st)
        pbuf = sb("pbuf", [P, 3, S], where=st)
        up_raw = sb("up_raw", [P, 2, PAIRS, P], where=st)
        up_hi = sb("up_hi", [P, 2, PAIRS, P], F32R, where=st)
        up_lo = sb("up_lo", [P, 2, PAIRS, P], F32R, where=st)
        gate = sb("gate", [P, HALF], where=st)
        mst = sb("mst", [P, HALF], where=st)
        row4 = sb("row4", [P, 2, 2], where=st)
        ngb = sb("ngb", [P, 2 * KT], where=st)
        nrm = pbuf[:, 2]
        pa_flat = pa[:, :, :].rearrange("p a s -> p (a s)")
        pb_flat = pb[:, :, :].rearrange("p a s -> p (a s)")

        fox_in = {n: sem("fox_in_" + n) for n in "qkvz"}
        fox_to = {"q": fq, "k": fk, "v": fv, "z": fz}
        ya_hi_done = sem("ya_hi_done")
        ya_ready = sem("ya_ready")
        up_loaded = [sem("up_loaded0"), sem("up_loaded1")]
        up_hi_done = sem("up_hi_done")
        up_ready = sem("up_ready")
        up_done = sem("up_done")
        up_free = sem("up_free")
        gate_act = sem("gate_act")
        gate_plus = sem("gate_plus")
        m_stored = sem("m_stored")
        fsq_done = sem("fsq_done")
        fsum_mm = sem("fsum_mm")
        fnorm_act = sem("fnorm_act")
        f_normed = sem("f_normed")
        z_act = sem("z_act")
        z_step = sem("z_step")
        v_turned = sem("v_turned")
        v_out = sem("v_out")
        hi_stacked = sem("hi_stacked")
        stacked = sem("stacked")
        c_loaded = sem("c_loaded")
        d_step = sem("d_step")
        score_mm = sem("score_mm")
        score_out = sem("score_out")
        p_exp = sem("p_exp")
        p_step = sem("p_step")
        pt_mm = sem("pt_mm")
        pt_act = sem("pt_act")
        pt_dve = sem("pt_dve")
        pv_mm = sem("pv_mm")
        of_out = sem("of_out")
        y_step = sem("y_step")
        y_stored = sem("y_stored")
        N3 = N2 + N_FOX
        ITEMS = 2 * NT
        UNITS = 4
        FILLS = (1, 1, 2, 1, 1, 1, 1, 1, 6, 2, 2, 2, 2, 1, 1, 1)

        def split_up_hi(act, p, slot):
            act.wait_ge(up_loaded[slot], 16 * p + 16)
            act.wait_ge(up_done, 4 * p)
            nc.scalar.activation(up_hi[:, slot], up_raw[:, slot], ACT.Copy).then_inc(up_hi_done, 1)

        def split_up_lo(dve, q, slot):
            dve.wait_ge(up_hi_done, q + 1)
            nc.vector.tensor_tensor(up_lo[:, slot], up_raw[:, slot], up_hi[:, slot].bitcast(F32),
                                    ALU.subtract).then_inc(up_ready, 1)

        def gate_exp(act, u, gate_col, psum, dst):
            act.wait_ge(pj_done, u + 1)
            alone(act)
            nc.scalar.activation(dst, psum, ACT.Exp, bias=ngb[:, ds(gate_col, 1)], scale=-1.0).then_inc(pj_free, 1)

        with nc.Block() as block:
            @block.sync
            def _(sp):
                def load_up(p):
                    for j in range(2):
                        sp.wait_ge(up_ready, 2 * p)
                        sp.dma_start(up_raw[:, j], up_view[0][:, :, ds((2 * p + j) * P, P)]).then_inc(up_loaded[j], 16)

                def load_fox(name, p):
                    part = "qkvz".index(name)
                    sp.dma_start(fox_to[name][:, :], fox_dram[ds((p + part * PAIRS) * P, P), :]).then_inc(fox_in[name], 16)

                def step(p, more):
                    n0 = 2 * p + N3
                    load_w(sp, n0 + 2, COL_GATE + 2 * P + 2 * P * p, 1)
                    if more:
                        load_w(sp, n0 + 3, COL_GATE + 3 * P + 2 * P * p, 0)
                        load_up(p + 1)
                        sp.wait_ge(stacked, 2 * p + 2)
                        sp.wait_ge(hi_stacked, 6 * p + 6)
                        load_fox("q", p + 1)
                        load_fox("k", p + 1)
                    sp.wait_ge(y_step, 2 * p + 2)
                    sp.dma_start(y_dram[ds(p * P, P), :], fz[:, :]).then_inc(y_stored, 16)
                    if more:
                        load_fox("v", p + 1)
                        sp.wait_ge(y_stored, 16 * p + 16)
                        load_fox("z", p + 1)

                for name in "qkvz":
                    load_fox(name, 0)
                load_up(0)
                load_w(sp, N3 + 1, COL_GATE + P, 0)
                with sp.Fori(0, PAIRS - 1) as p:
                    step(p, True)
                step(PAIRS - 1, False)

            @block.gpsimd
            def _(pool):
                pool.wait_ge(ya_ready, PAIRS)
                with pool.Fori(0, PAIRS) as p:
                    for hh in range(2):
                        pool.dma_start(c_all[:, :], rows_dram[2, ds(2 * p + hh, 1), :].rearrange("a s -> (a s)")
                                       .partition_broadcast(P)).then_inc(c_loaded, 16)
                        pool.wait_ge(c_loaded, 32 * p + 16 * hh + 16)
                        for b in range(NT):
                            i = NT * hh + b
                            w = P * (b + 1)
                            pool.wait_ge(score_out, ITEMS * p + max(i - 1, 0))
                            c_i = c_tok.rearrange("p t h -> p (t h)")[:, ds(2 * p + hh + H * b, 1)].broadcast_to([P, w])
                            nc.gpsimd.tensor_tensor(dmat[:, i % 2, 0:w], c_all[:, 0:w], c_i, ALU.subtract).then_inc(d_step, 1)
                            pool.wait_ge(d_step, 2 * ITEMS * p + 2 * i + 1)
                            alone(pool)
                            nc.gpsimd.affine_select(dmat[:, i % 2, w - P:w], dmat[:, i % 2, w - P:w], pattern=[[-1, P]], base=0,
                                                    channel_multiplier=1, compare_op=ALU.is_ge,
                                                    fill=-NEG).then_inc(d_step, 1)

            @block.scalar
            def _(act):
                for k in range(PAIRS):
                    nc.scalar.activation(ya_hi[:, k], zg[:, k], ACT.Copy).then_inc(ya_hi_done, 1)

                def squares_qk(p):
                    for n, (src, name) in enumerate(((fq, "q"), (fk, "k"))):
                        act.wait_ge(fox_in[name], 16 * p + 16)
                        if not isinstance(p, int):
                            act.wait_ge(pt_mm, ITEMS * p)
                        nc.scalar.activation(pbuf[:, n], src[:, :], ACT.Square).then_inc(fsq_done, 1)

                def step(p, more):
                    n0 = 2 * p + N3
                    u0 = 2 * n0

                    def sigmoid_gate(n):
                        act.wait_ge(gate_plus, UNITS * p + n + 1)
                        nc.scalar.activation(gate[:, :], gate[:, :], ACT.Ln).then_inc(gate_act, 1)
                        act.wait_ge(gate_act, 2 * UNITS * p + 2 * n + 1)
                        nc.scalar.activation(gate[:, :], gate[:, :], ACT.Exp, scale=-1.0).then_inc(gate_act, 1)

                    def exp_unit(n):
                        act.wait_ge(up_free, UNITS * p + n)
                        gate_exp(act, u0 + n, 2 * p + n // 2, pj[:, 0], gate[:, :])

                    def store_unit(n):
                        act.wait_ge(up_free, UNITS * p + n + 1)
                        act.dma_start(m_dram[ds((2 * p + n // 2) * P, P), HALF * (n % 2):HALF * (n % 2) + HALF],
                                      mst[:, :]).then_inc(m_stored, 16)

                    def norms(n, dst, sums):
                        act.wait_ge(fsum_mm, 3 * p + n + 1)
                        nc.scalar.activation(dst, sums, ACT.Ln, bias=eps_t, scale=1.0 / DH).then_inc(fnorm_act, 1)
                        act.wait_ge(fnorm_act, 6 * p + 2 * n + 1)
                        nc.scalar.activation(dst, dst, ACT.Exp, scale=-0.5).then_inc(fnorm_act, 1)

                    def stack(hh):
                        rows = slice(DH * hh, DH * hh + DH)
                        if hh == 0:
                            act.wait_ge(f_normed, 2 * p + 1)
                        nc.scalar.activation(q_st[rows], fq[rows], ACT.Copy).then_inc(hi_stacked, 1)
                        if hh == 0:
                            act.wait_ge(f_normed, 2 * p + 2)
                        for half in (hh, 1 - hh):
                            nc.scalar.activation(k_hi[DH * half:DH * half + DH], fk[rows], ACT.Copy).then_inc(hi_stacked, 1)

                    def take_turned(i):
                        w = min(i % NT + 1, 4)
                        act.wait_ge(pt_mm, ITEMS * p + i + 1)
                        act.wait_ge(pv_mm, ITEMS * p + i)
                        nc.scalar.activation(ptb[:, 0:w], pb[:, 0, 0:P * w].rearrange("p (n c) -> p n c", c=P),
                                             ACT.Copy).then_inc(pt_act, 1)

                    def take_out(i):
                        hh, b = divmod(i, NT)
                        rows = slice(DH * hh, DH * hh + DH)
                        act.wait_ge(pv_mm, ITEMS * p + i + 1)
                        nc.scalar.activation(fv[rows, P * b:P * b + P], pc[rows, i % 2, 0:P], ACT.Copy).then_inc(of_out, 1)

                    split_up_hi(act, p, 0)
                    norms(0, pbuf[:, 0], pa_flat)
                    norms(1, pbuf[:, 1], pb_flat)
                    stack(0)
                    exp_unit(0)
                    act.wait_ge(v_turned, p + 1)
                    for b in range(2):
                        nc.scalar.activation(v_tok[:, 4 * b:4 * b + 4], pc[:, b].rearrange("p (n c) -> p n c", c=P),
                                             ACT.Copy).then_inc(v_out, 1)
                    for i in range(ITEMS):
                        hh, b = divmod(i, NT)
                        w = P * (b + 1)
                        if i >= 2:
                            take_turned(i - 2)
                        if i == NT:
                            act.wait_ge(stacked, 2 * p + 1)
                            act.wait_ge(score_mm, ITEMS * p + NT)
                            stack(1)
                        act.wait_ge(score_out, ITEMS * p + i + 1)
                        nc.scalar.activation(pbuf[:, i % 3, 0:w], pbuf[:, i % 3, 0:w], ACT.Exp, bias=row4[:, i % 2, 0:1],
                                             scale=-1.0, accum_out=row4[:, i % 2, 1:2]).then_inc(p_exp, 1)
                        if i >= 2:
                            take_out(i - 2)
                        if i == 0:
                            sigmoid_gate(0)
                        if i == 1:
                            split_up_hi(act, p, 1)
                        if i == 2:
                            store_unit(0)
                            split_hi(act, n0 + 1, p + (N3 + 1) // 2, 0)
                        if i == 3:
                            act.wait_ge(fox_in["z"], 16 * p + 16)
                            nc.scalar.activation(sqf[:, :], fz[:, :], ACT.Exp, scale=-1.0).then_inc(z_act, 1)
                        if i == 4:
                            act.wait_ge(z_step, 2 * p + 1)
                            nc.scalar.activation(sqf[:, :], sqf[:, :], ACT.Ln).then_inc(z_act, 1)
                        if i == 5:
                            act.wait_ge(z_act, 3 * p + 2)
                            nc.scalar.activation(sqf[:, :], sqf[:, :], ACT.Exp, scale=-1.0).then_inc(z_act, 1)
                        if i == 5:
                            exp_unit(1)
                        if i == 7:
                            sigmoid_gate(1)
                        if i == 9:
                            store_unit(1)
                        if i == 9:
                            split_hi(act, n0 + 2, p + (N3 + 1) // 2, 1)
                        if i == 11:
                            exp_unit(2)
                        if i == 12:
                            sigmoid_gate(2)
                        if i == 14:
                            store_unit(2)
                    for i in (ITEMS - 2, ITEMS - 1):
                        take_turned(i)
                        take_out(i)
                    act.wait_ge(of_out, ITEMS * p + ITEMS)
                    act.wait_ge(z_step, 2 * p + 2)
                    nc.scalar.activation(sqf[:, :], fv[:, :], ACT.Square).then_inc(fsq_done, 1)
                    if more:
                        squares_qk(p + 1)
                    norms(2, nrm, pa_flat)
                    exp_unit(3)
                    sigmoid_gate(3)
                    store_unit(3)

                squares_qk(0)
                act.wait_ge(ya_ready, PAIRS)
                with act.Fori(0, PAIRS - 1) as p:
                    step(p, True)
                step(PAIRS - 1, False)

            @block.vector
            def _(dve):
                for k in range(PAIRS):
                    dve.wait_ge(ya_hi_done, k + 1)
                    nc.vector.tensor_tensor(ya_lo[:, k], zg[:, k], ya_hi[:, k].bitcast(F32), ALU.subtract).then_inc(ya_ready, 1)
                nc.vector.tensor_scalar(ngb[:, :], cst[:, 64:64 + 2 * KT], -1.0, None, ALU.mult)
                with dve.Fori(0, PAIRS) as p:
                    n0 = 2 * p + N3
                    u0 = 2 * n0

                    def plus_unit(n):
                        dve.wait_ge(pj_free, u0 + n + 3)
                        nc.vector.tensor_scalar(gate[:, :], gate[:, :], LN_MAX, 1.0, ALU.min, ALU.add).then_inc(gate_plus, 1)

                    def gated_unit(n):
                        dve.wait_ge(gate_act, 2 * UNITS * p + 2 * n + 2)
                        dve.wait_ge(up_done, UNITS * p + n + 1)
                        dve.wait_ge(m_stored, 16 * UNITS * p + 16 * n)
                        nc.vector.tensor_tensor(mst[:, :], pj[:, 1], gate[:, :], ALU.mult).then_inc(up_free, 1)

                    def stack(hh):
                        rows = slice(DH * hh, DH * hh + DH)
                        other = slice(DH * (1 - hh), DH * (1 - hh) + DH)
                        h0 = 6 * p + 3 * hh
                        dve.wait_ge(hi_stacked, h0 + 1)
                        nc.vector.tensor_tensor(q_st[other], fq[rows], q_st[rows].bitcast(F32), ALU.subtract)
                        dve.wait_ge(hi_stacked, h0 + 2)
                        nc.vector.tensor_tensor(k_lo[rows], fk[rows], k_hi[rows].bitcast(F32), ALU.subtract)
                        nc.vector.tensor_tensor(k_lo[other], fk[rows], k_hi[rows].bitcast(F32),
                                                ALU.subtract).then_inc(stacked, 1)

                    def take_turned(i):
                        b = i % NT
                        if b < 4:
                            return
                        dve.wait_ge(pt_mm, ITEMS * p + i + 1)
                        dve.wait_ge(pv_mm, ITEMS * p + i)
                        nc.vector.tensor_copy(ptb[:, 4:b + 1], pb[:, 1, 0:P * (b - 3)].rearrange("p (n c) -> p n c", c=P)
                                              ).then_inc(pt_dve, 1)

                    def normalise(i):
                        w = P * (i % NT + 1)
                        dve.wait_ge(p_exp, ITEMS * p + i + 1)
                        nc.vector.reciprocal(row4[:, i % 2, 1:2], row4[:, i % 2, 1:2]).then_inc(p_step, 1)
                        dve.wait_ge(p_step, 2 * ITEMS * p + 2 * i + 1)
                        nc.vector.tensor_scalar(pbuf[:, i % 3, 0:w], pbuf[:, i % 3, 0:w], row4[:, i % 2, 1:2], None,
                                                ALU.mult).then_inc(p_step, 1)

                    split_up_lo(dve, 2 * p, 0)
                    for n, (t, name) in enumerate(((fq, "q"), (fk, "k"))):
                        dve.wait_ge(fnorm_act, 6 * p + 2 * n + 2)
                        nc.vector.scalar_tensor_tensor(t[:, :], t[:, :], fox_nw[name], pbuf[:, n], ALU.mult,
                                                       ALU.mult).then_inc(f_normed, 1)
                    stack(0)
                    plus_unit(0)
                    for i in range(ITEMS):
                        hh, b = divmod(i, NT)
                        w = P * (b + 1)
                        if i >= 2:
                            take_turned(i - 2)
                        if i == NT:
                            stack(1)
                        if i == 2:
                            dve.wait_ge(y_step, 2 * p)
                        dve.wait_ge(score_mm, ITEMS * p + i + 1)
                        dve.wait_ge(d_step, 2 * ITEMS * p + 2 * i + 2)
                        dve.wait_ge(pt_mm, ITEMS * p + max(i - 2, 0))
                        alone(dve)
                        nc.vector.tensor_tensor_reduce(pbuf[:, i % 3, 0:w], dmat[:, i % 2, 0:w], pa_flat[:, 0:w], 1.0, 3e38,
                                                       ALU.add, ALU.min, row4[:, i % 2, 0:1]).then_inc(score_out, 1)
                        if i == 1:
                            gated_unit(0)
                        if i == 2:
                            split_up_lo(dve, 2 * p + 1, 1)
                        if i == 3:
                            split_lo(dve, n0 + 1, 0)
                        if i == 4:
                            dve.wait_ge(z_act, 3 * p + 1)
                            nc.vector.tensor_scalar(sqf[:, :], sqf[:, :], LN_MAX, 1.0, ALU.min, ALU.add).then_inc(z_step, 1)
                        if i == 6:
                            plus_unit(1)
                        if i == 7:
                            dve.wait_ge(z_act, 3 * p + 3)
                            nc.vector.scalar_tensor_tensor(fz[:, :], fz[:, :], fox_nw["o"], sqf[:, :], ALU.mult,
                                                           ALU.mult).then_inc(z_step, 1)
                        if i == 8:
                            gated_unit(1)
                        if i == 10:
                            split_lo(dve, n0 + 2, 1)
                        if i == 12:
                            plus_unit(2)
                        if i == 13:
                            gated_unit(2)
                        normalise(i)
                    take_turned(ITEMS - 2)
                    take_turned(ITEMS - 1)
                    dve.wait_ge(fnorm_act, 6 * p + 6)
                    nc.vector.tensor_tensor(nrm, fv[:, :], nrm, ALU.mult).then_inc(y_step, 1)
                    dve.wait_ge(y_step, 2 * p + 1)
                    nc.vector.tensor_tensor(fz[:, :], fz[:, :], nrm, ALU.mult).then_inc(y_step, 1)
                    plus_unit(3)
                    gated_unit(3)

            @block.tensor
            def _(pe):
                with pe.Fori(0, PAIRS) as p:
                    n0 = 2 * p + N3
                    done = [0]

                    def fill(count):
                        for _ in range(count):
                            unit, k = divmod(done[0], KT + PAIRS)
                            tile, half = divmod(unit, 2)
                            if k < KT:
                                project(pe, n0 + tile, 1 - tile, half, k, banks=1)
                            else:
                                project_up(pe, 2 * p + tile, tile, half, k - KT, ya_hi, ya_lo, pj[:, 1],
                                           up_hi, up_lo)
                            done[0] += 1

                    def head_sums(n, sums, src):
                        pe.wait_ge(fsq_done, 3 * p + n + 1)
                        for half in range(2):
                            last = nc.tensor.matmul(sums[:, half], blk_ones[:, :], src[:, HALF * half:HALF * half + HALF],
                                                    start=True, stop=True)
                        last.then_inc(fsum_mm, 1)

                    def turn(i):
                        pe.wait_ge(p_step, 2 * ITEMS * p + 2 * i + 2)
                        for b in range(i % NT + 1):
                            last = nc.tensor.transpose(pb[:, b // 4, P * (b % 4):P * (b % 4) + P],
                                                       pbuf[:, i % 3, P * b:P * b + P], ident[:, :])
                        last.then_inc(pt_mm, 1)

                    def values(i):
                        hh, b = divmod(i, NT)
                        rows = slice(DH * hh, DH * hh + DH)
                        pe.wait_ge(pt_act, ITEMS * p + i + 1)
                        if b >= 4:
                            pe.wait_ge(pt_dve, NT * p + 4 * hh + b - 3)
                        pe.wait_ge(of_out, ITEMS * p + max(i - 1, 0))
                        for j in range(b + 1):
                            last = nc.tensor.matmul(pc[rows, i % 2, 0:P], v_tok[:, j, rows], ptb[:, j],
                                                    start=(j == 0), stop=(j == b))
                        last.then_inc(pv_mm, 1)

                    fill(2)
                    head_sums(0, pa, pbuf[:, 0])
                    pe.wait_ge(pt_act, ITEMS * p)
                    pe.wait_ge(pt_dve, NT * p)
                    head_sums(1, pb, pbuf[:, 1])
                    fill(3)
                    pe.wait_ge(ya_ready, PAIRS)
                    pe.wait_ge(fox_in["v"], 16 * p + 16)
                    pe.wait_ge(of_out, ITEMS * p)
                    for t in range(NT):
                        last = nc.tensor.transpose(pc[:, t // 4, P * (t % 4):P * (t % 4) + P], fv[:, P * t:P * t + P],
                                                   ident[:, :])
                    last.then_inc(v_turned, 1)
                    fill(9)
                    pe.wait_ge(fnorm_act, 6 * p + 3)
                    pe.wait_ge(v_out, 2 * p + 2)

                    def scores(i):
                        hh, b = divmod(i, NT)
                        pe.wait_ge(stacked, 2 * p + hh + 1)
                        pe.wait_ge(hi_stacked, 6 * p + 3 * hh + 3)
                        pe.wait_ge(score_out, ITEMS * p + i)
                        w = P * (b + 1)
                        for lo in range(0, w, HALF):
                            cols = slice(lo, min(w, lo + HALF))
                            nc.tensor.matmul(pa_flat[:, cols], q_st[:, P * b:P * b + P], k_hi[:, cols], start=True, stop=False)
                            last = nc.tensor.matmul(pa_flat[:, cols], q_st[:, P * b:P * b + P], k_lo[:, cols],
                                                    start=False, stop=True)
                        last.then_inc(score_mm, 1)

                    for i in range(ITEMS):
                        if i >= 2:
                            turn(i - 2)
                        if i != NT:
                            scores(i)
                        fill(FILLS[i])
                        if i >= 2:
                            values(i - 2)
                        if i == NT:
                            scores(i)
                    turn(ITEMS - 2)
                    fill(1)
                    values(ITEMS - 2)
                    turn(ITEMS - 1)
                    fill(2)
                    values(ITEMS - 1)
                    fill(2)
                    pe.wait_ge(score_out, ITEMS * p + ITEMS)
                    head_sums(2, pa, sqf)
                    fill(3)
                    pe.wait_ge(fnorm_act, 6 * p + 5)
                    assert done[0] == UNITS * (KT + PAIRS)

        st.close()

        wo_raw = sb("wo_raw", [P, 2, D])
        merged = sb("merged", [P, KT, S])
        st = ctx.enter_context(ExitStack())
        yb = sb("yb", [P, PAIRS, S], where=st)
        yb_hi = sb("yb_hi", [P, PAIRS, S], F32R, where=st)
        yb_lo = sb("yb_lo", [P, PAIRS, S], F32R, where=st)
        up_raw = sb("up_raw_b", [P, 2, PAIRS, P], where=st)
        up_hi = sb("up_hi_b", [P, 2, PAIRS, P], F32R, where=st)
        up_lo = sb("up_lo_b", [P, 2, PAIRS, P], F32R, where=st)
        ma = sb("ma", [P, 2, S], where=st)
        gates = sb("gates", [P, 2, HALF], where=st)
        ngb = sb("ngb_b", [P, 2 * KT], where=st)

        yb_loaded = [sem(f"yb_loaded{k}") for k in range(PAIRS)]
        yb_hi_done = sem("yb_hi_done")
        yb_ready = sem("yb_ready")
        ngb_done = sem("ngb_done")
        upb_loaded = [sem("upb_loaded0"), sem("upb_loaded1")]
        ma_loaded = [sem("ma_loaded0"), sem("ma_loaded1")]
        gate2_act = sem("gate2_act")
        gate2_plus = sem("gate2_plus")
        up2_read = sem("up2_read")
        merge_done = sem("merge_done")
        wo_loaded = [sem("wo_loaded0"), sem("wo_loaded1")]
        N4 = N3 + KT
        NTILES = N4 + KT
        UP0 = 2 * UNITS * PAIRS // 2

        with nc.Block() as block:
            @block.sync
            def _(sp):
                sp.wait_ge(m_stored, 16 * UNITS * PAIRS)
                sp.wait_ge(y_stored, 16 * PAIRS)
                for k in range(PAIRS):
                    sp.dma_start(yb[:, k], y_dram[P * k:P * k + P, :]).then_inc(yb_loaded[k], 16)

                def step(i, weights):
                    for j in range(2):
                        sp.wait_ge(up_ready, 2 * i + 2 * PAIRS)
                        sp.dma_start(up_raw[:, j], up_view[1][:, :, ds((2 * i + j) * P, P)]).then_inc(upb_loaded[j], 16)
                        sp.wait_ge(merge_done, 4 * i)
                        sp.dma_start(ma[:, j], m_dram[ds((2 * i + j) * P, P), :]).then_inc(ma_loaded[j], 16)
                        if weights > j:
                            load_w(sp, N4 + 1 + 2 * i + j, COL_GATE + (KT + 1 + j) * P + 2 * P * i, j)

                with sp.Fori(0, KT // 2 - 1) as i:
                    step(i, 2)
                step(KT // 2 - 1, 1)
                for k in range(2):
                    sp.dma_start(wo_raw[:, k], w_out[0, P * k:P * k + P, :]).then_inc(wo_loaded[k], 16)

            @block.scalar
            def _(act):
                for k in range(PAIRS):
                    act.wait_ge(yb_loaded[k], 16)
                    nc.scalar.activation(yb_hi[:, k], yb[:, k], ACT.Copy).then_inc(yb_hi_done, 1)
                act.wait_ge(ngb_done, 1)

                def step(i, more):
                    for j in range(2):
                        act.wait_ge(upb_loaded[j], 16 * i + 16)
                        act.wait_ge(up_done, 4 * i + UP0)
                        nc.scalar.activation(up_hi[:, j], up_raw[:, j], ACT.Copy).then_inc(up_hi_done, 1)
                    for j in range(2):
                        n = 2 * i + j + N4
                        if more > j:
                            split_hi(act, n + 1, i + (N4 + 1) // 2, j)
                        for half in range(2):
                            q = 4 * i + 2 * j + half
                            act.wait_ge(up2_read, q - 1 if j or half else 4 * i)
                            act.wait_ge(pj_done, 2 * n + half + 1)
                            alone(act)
                            nc.scalar.activation(gates[:, half], pj[:, half], ACT.Exp, bias=ngb[:, ds(2 * i + j + KT, 1)],
                                                 scale=-1.0).then_inc(pj_free, 1)
                            act.wait_ge(gate2_plus, q + 1)
                            nc.scalar.activation(gates[:, half], gates[:, half], ACT.Ln).then_inc(gate2_act, 1)
                            act.wait_ge(gate2_act, 2 * q + 1)
                            nc.scalar.activation(gates[:, half], gates[:, half], ACT.Exp, scale=-1.0).then_inc(gate2_act, 1)

                with act.Fori(0, KT // 2 - 1) as i:
                    step(i, 2)
                step(KT // 2 - 1, 1)

            @block.vector
            def _(dve):
                nc.vector.tensor_scalar(ngb[:, :], cst[:, 64:64 + 2 * KT], -1.0, None, ALU.mult).then_inc(ngb_done, 1)
                for k in range(PAIRS):
                    dve.wait_ge(yb_hi_done, k + 1)
                    nc.vector.tensor_tensor(yb_lo[:, k], yb[:, k], yb_hi[:, k].bitcast(F32), ALU.subtract).then_inc(yb_ready, 1)

                def step(i, more):
                    for j in range(2):
                        dve.wait_ge(up_hi_done, 2 * i + j + 1 + 2 * PAIRS)
                        nc.vector.tensor_tensor(up_lo[:, j], up_raw[:, j], up_hi[:, j].bitcast(F32),
                                                ALU.subtract).then_inc(up_ready, 1)
                    for j in range(2):
                        n = 2 * i + j + N4
                        if more > j:
                            split_lo(dve, n + 1, j)
                        for half in range(2):
                            q = 4 * i + 2 * j + half
                            dve.wait_ge(pj_free, 2 * n + half + 3)
                            nc.vector.tensor_scalar(gates[:, half], gates[:, half], LN_MAX, 1.0, ALU.min,
                                                    ALU.add).then_inc(gate2_plus, 1)
                            dve.wait_ge(gate2_act, 2 * q + 2)
                            dve.wait_ge(up_done, q + UP0 + 1)
                            nc.vector.tensor_tensor(gates[:, half], pa[:, half], gates[:, half], ALU.mult).then_inc(up_free, 1)
                            dve.wait_ge(up_free, q + UP0 + 1)
                            dve.wait_ge(ma_loaded[j], 16 * i + 16)
                            cols = slice(HALF * half, HALF * half + HALF)
                            nc.vector.tensor_tensor(merged[:, ds(2 * i + j, 1), cols].rearrange("p a s -> p (a s)"),
                                                    ma[:, j, cols], gates[:, half], ALU.add).then_inc(up2_read, 1)
                    dve.wait_ge(up2_read, 4 * i + 4)
                    dve.sem_inc(merge_done, 4)

                with dve.Fori(0, KT // 2 - 1) as i:
                    step(i, 2)
                step(KT // 2 - 1, 1)

            @block.tensor
            def _(pe):
                with pe.Fori(0, KT // 2) as i:
                    for j in range(2):
                        for half in range(2):
                            for k in range(KT):
                                project(pe, 2 * i + j + N4, 1 - j, half, k)
                        for half in range(2):
                            for k in range(PAIRS):
                                if j == 0 and half == 0:
                                    pe.wait_ge(yb_ready, k + 1)
                                project_up(pe, 2 * i + j + 2 * PAIRS, j, half, k, yb_hi, yb_lo, pa[:, half], up_hi, up_lo)
        st.close()

        st = ctx.enter_context(ExitStack())
        o_hi = sb("o_hi", [P, KT, D], F32R, where=st)
        o_lo = sb("o_lo", [P, KT, D], F32R, where=st)
        xo = w_raw[:, :, :, :].rearrange("p a k n -> p a (k n)")
        fn_bc = sb("fn_bc", [P, D], where=st)
        fstat = sb("fstat", [P, 2], where=st)
        m_hi, m_lo = h_hi, h_lo
        banks = (pj, pa, pb, pc)

        wo_hi_done = sem("wo_hi_done")
        wo_ready = sem("wo_ready")
        xo_loaded = [sem("xo_loaded0"), sem("xo_loaded1")]
        fn_loaded = sem("fn_loaded")
        out_mm = sem("out_mm")
        sum_done = sem("sum_done")
        fsq2_done = sem("fsq2_done")
        final_done = sem("final_done")
        out_stored = [sem("out_stored0"), sem("out_stored1")]

        with nc.Block() as block:
            @block.sync
            def _(sp):
                sp.dma_start(fn_bc[:, :], final_norm_w.partition_broadcast(P)).then_inc(fn_loaded, 16)
                for k in range(2, KT):
                    sp.wait_ge(wo_ready, k - 1)
                    sp.dma_start(wo_raw[:, k % 2], w_out[0, P * k:P * k + P, :]).then_inc(wo_loaded[k % 2], 16)
                for t in range(NT):
                    if t >= 2:
                        sp.wait_ge(out_stored[t % 2], 16 * (t // 2))
                    sp.dma_start(xo[:, t % 2], x[0, P * t:P * t + P, :]).then_inc(xo_loaded[t % 2], 16)

            @block.scalar
            def _(act):
                for k in range(KT):
                    nc.scalar.activation(m_hi[:, k], merged[:, k], ACT.Copy).then_inc(wo_hi_done, 1)
                    act.wait_ge(wo_loaded[k % 2], 16 * (k // 2 + 1))
                    nc.scalar.activation(o_hi[:, k], wo_raw[:, k % 2], ACT.Copy).then_inc(wo_hi_done, 1)
                for t in range(NT):
                    s = t % 2
                    act.wait_ge(sum_done, 2 * t + 2)
                    if t:
                        act.wait_ge(fsq2_done, 3 * t)
                    else:
                        act.wait_ge(wo_ready, KT)
                    nc.scalar.activation(merged[:, 0], xo[:, s], ACT.Square,
                                         accum_out=fstat[:, s:s + 1]).then_inc(fsq2_done, 1)
                    act.wait_ge(fsq2_done, 3 * t + 1)
                    nc.scalar.activation(fstat[:, s:s + 1], fstat[:, s:s + 1], ACT.Ln, bias=eps_t,
                                         scale=1.0 / D).then_inc(fsq2_done, 1)
                    act.wait_ge(fsq2_done, 3 * t + 2)
                    nc.scalar.activation(fstat[:, s:s + 1], fstat[:, s:s + 1], ACT.Exp, scale=-0.5).then_inc(fsq2_done, 1)
                    act.wait_ge(final_done, t + 1)
                    act.dma_start(out[0, P * t:P * t + P, :], xo[:, s]).then_inc(out_stored[s], 16)
                for s in range(2):
                    act.wait_ge(out_stored[s], 16 * (NT // 2))

            @block.vector
            def _(dve):
                for k in range(KT):
                    dve.wait_ge(wo_hi_done, 2 * k + 1)
                    nc.vector.tensor_tensor(m_lo[:, k], merged[:, k], m_hi[:, k].bitcast(F32), ALU.subtract)
                    dve.wait_ge(wo_hi_done, 2 * k + 2)
                    nc.vector.tensor_tensor(o_lo[:, k], wo_raw[:, k % 2], o_hi[:, k].bitcast(F32),
                                            ALU.subtract).then_inc(wo_ready, 1)
                dve.wait_ge(fn_loaded, 16)
                for t in range(NT):
                    s = t % 2
                    dve.wait_ge(xo_loaded[s], 16 * (t // 2 + 1))
                    for half in range(2):
                        cols = slice(HALF * half, HALF * half + HALF)
                        dve.wait_ge(out_mm, 2 * t + half + 1)
                        nc.vector.tensor_tensor(xo[:, s, cols], xo[:, s, cols], banks[t % 4][:, half],
                                                ALU.add).then_inc(sum_done, 1)
                    dve.wait_ge(fsq2_done, 3 * t + 3)
                    nc.vector.scalar_tensor_tensor(xo[:, s], xo[:, s], fstat[:, s:s + 1], fn_bc[:, :], ALU.mult,
                                                   ALU.mult).then_inc(final_done, 1)

            @block.tensor
            def _(pe):
                def part(t, half, k):
                    o = banks[t % 4][:, half]
                    rows, cols = slice(P * t, P * t + P), slice(HALF * half, HALF * half + HALF)
                    nc.tensor.matmul(o, m_hi[:, k, rows], o_hi[:, k, cols], start=(k == 0), stop=False)
                    nc.tensor.matmul(o, m_hi[:, k, rows], o_lo[:, k, cols], start=False, stop=False)
                    last = nc.tensor.matmul(o, m_lo[:, k, rows], o_hi[:, k, cols], start=False, stop=(k == KT - 1))
                    if k == KT - 1:
                        last.then_inc(out_mm, 1)

                for k in range(KT):
                    pe.wait_ge(wo_ready, k + 1)
                    for t in range(4):
                        for half in range(2):
                            part(t, half, k)
                for t in range(4, NT):
                    for half in range(2):
                        pe.wait_ge(sum_done, 2 * (t - 4) + half + 1)
                        for k in range(KT):
                            part(t, half, k)


_INS = ['x', 'norm_w', 'w_in', 'gate_b', 'conv_w', 'a_log', 'dt_bias', 'gdn_norm_w', 'f_bias', 'fox_qn_w', 'fox_kn_w',
        'fox_on_w', 'w_up_gdn', 'w_up_fox', 'w_out', 'final_norm_w']


def kernel(**inputs):
    import numpy as _np
    import concourse.bacc as _bacc
    from concourse import mybir as _mybir
    from concourse.bass_utils import run_bass_kernel_spmd as _run

    nc = _bacc.Bacc("TRN2", target_bir_lowering=False, num_devices=1)
    arrays, args = {}, []
    for name in _INS:
        a = _np.ascontiguousarray(inputs[name])
        arrays[f"in_{name}"] = a
        args.append(nc.dram_tensor(f"in_{name}", a.shape, _mybir.dt.from_np(a.dtype), kind="ExternalInput").ap())
    x = arrays["in_x"]
    args.append(nc.dram_tensor("out_0", x.shape, _mybir.dt.from_np(x.dtype), kind="ExternalOutput").ap())
    program(nc, *args)
    r = _run(nc, [arrays], core_ids=[0])
    return r.results[0]["out_0"]
```
